# Optimizing a Trainium2 kernel written in Bass

```python
import math
import jax, jax.numpy as jnp
from jax import lax
import numpy as np

D_MODEL = 1024
BATCH = 1
SEQ = 256
DEPTH = 1
DEC_BATCH = 8
DEC_SEQ = 8
PAST_LEN = 2048
PAGE_SIZE = 128

HG_W = D_MODEL // 2
HG_DK = 128
HG_DV = 128
HG_H = HG_W // HG_DK
HG_CHUNK = 64
RW_W = D_MODEL - HG_W
RW_N = 64
RW_H = RW_W // RW_N
RW_DECAY_LORA = 64
RW_A_LORA = 64
RW_G_LORA = 128
HG_COLS = 2 * HG_H * HG_DK + 2 * HG_H * HG_DV
RW_COLS = 3 * RW_W + RW_DECAY_LORA + RW_A_LORA + RW_G_LORA
MIX_W = HG_H * HG_DV + RW_W
N_EXPERTS = 32
TOP_K = 4
D_FF = D_MODEL
SWIGLU_LIMIT = 7.0
SWIGLU_ALPHA = 1.702
MOE_BLOCK = 128
NORM_EPS = 1e-6
RW_GN_EPS = 64e-5

kernel_name = "hymba_style_hgrn2_rwkv7_moe_step"

F32 = jnp.float32

def rmsnorm(x, g):
    xf = x.astype(F32)
    y = xf * lax.rsqrt(jnp.mean(xf * xf, axis=-1, keepdims=True) + NORM_EPS)
    return (y * g.astype(F32)).astype(x.dtype)

def hgrn2_mix(q, f_pre, i_in, g_in, lb, s0, gn_w):
    B, T, _ = q.shape
    C = math.gcd(HG_CHUNK, T)
    NC = T // C
    qf = jax.nn.silu(q.astype(F32))
    f = lb + (1.0 - lb) * jax.nn.sigmoid(f_pre.astype(F32))
    log_f = jnp.log(f)
    k = 1.0 - f

    def to_chunks(t, d):
        return t.reshape(B, NC, C, HG_H, d).transpose(1, 0, 3, 2, 4)

    mask = jnp.tril(jnp.ones((C, C), dtype=bool))

    def step(S, inp):
        qc, kc, lfc, ic = inp
        G = jnp.cumsum(lfc, axis=2)
        o_inter = jnp.einsum('bhtk,bhkv->bhtv', qc * jnp.exp(G), S)
        diff = G[:, :, :, None, :] - G[:, :, None, :, :]
        decay = jnp.exp(jnp.where(mask[:, :, None], diff, -jnp.inf))
        A = jnp.einsum('bhtk,bhtsk,bhsk->bhts', qc, decay, kc)
        o = o_inter + jnp.einsum('bhts,bhsv->bhtv', A, ic)
        G_last = G[:, :, -1:, :]
        S = jnp.exp(G_last[:, :, 0, :])[..., None] * S + jnp.einsum(
            'bhsk,bhsv->bhkv', kc * jnp.exp(G_last - G), ic)
        return S, o

    S, o = lax.scan(step, s0.astype(F32),
                    (to_chunks(qf, HG_DK), to_chunks(k, HG_DK), to_chunks(log_f, HG_DK),
                     to_chunks(i_in.astype(F32), HG_DV)))
    o = o.transpose(1, 0, 3, 2, 4).reshape(B, T, HG_H, HG_DV)
    o = o * lax.rsqrt(jnp.mean(o * o, axis=-1, keepdims=True) + NORM_EPS) * gn_w.astype(F32)
    o = o * jax.nn.silu(g_in.astype(F32).reshape(B, T, HG_H, HG_DV))
    return o.reshape(B, T, HG_H * HG_DV), S

def rwkv7_mix(p, p_prev, s0, mu, w0, w2, a0, a2, g2, k_k, k_a, r_k, lnx_w, lnx_b):
    B, T, _ = p.shape
    p = p.astype(F32)
    p_shift = jnp.concatenate([p_prev.astype(F32)[:, None, :], p[:, :-1]], axis=1)
    pm = p + (p_shift - p) * mu
    o1, o2, o3 = RW_W, 2 * RW_W, 3 * RW_W
    o4 = o3 + RW_DECAY_LORA
    o5 = o4 + RW_A_LORA
    r, k, v = pm[..., :o1], pm[..., o1:o2], pm[..., o2:o3]
    w_lo, a_lo, g_lo = pm[..., o3:o4], pm[..., o4:o5], pm[..., o5:]
    log_w = -jax.nn.softplus(-(w0 + jnp.tanh(w_lo) @ w2)) - 0.5
    decay = jnp.exp(-jnp.exp(log_w))
    a = jax.nn.sigmoid(a0 + a_lo @ a2)
    g = jax.nn.sigmoid(g_lo) @ g2

    def heads(t):
        return t.reshape(B, T, RW_H, RW_N)

    kk = heads(k * k_k)
    kk = kk / jnp.maximum(jnp.sqrt(jnp.sum(kk * kk, axis=-1, keepdims=True)), 1e-12)
    k = k * (1.0 + (a - 1.0) * k_a)
    r_h, k_h, v_h, w_h, a_h = heads(r), heads(k), heads(v), heads(decay), heads(a)

    def step(S, inp):
        r_t, w_t, k_t, v_t, kk_t, a_t = inp
        sa = jnp.einsum('bhvk,bhk->bhv', S, -kk_t)
        S = (S * w_t[:, :, None, :] + sa[..., None] * (kk_t * a_t)[:, :, None, :]
             + v_t[..., None] * k_t[:, :, None, :])
        return S, jnp.einsum('bhvk,bhk->bhv', S, r_t)

    def tm(t):
        return jnp.swapaxes(t, 0, 1)

    S, y = lax.scan(step, s0.astype(F32), (tm(r_h), tm(w_h), tm(k_h), tm(v_h), tm(kk), tm(a_h)))
    y = tm(y)
    mean = jnp.mean(y, axis=-1, keepdims=True)
    var = jnp.mean(jnp.square(y - mean), axis=-1, keepdims=True)
    y = ((y - mean) * lax.rsqrt(var + RW_GN_EPS)).reshape(B, T, RW_W) * lnx_w + lnx_b
    bonus = jnp.sum(r_h * k_h * r_k, axis=-1, keepdims=True) * v_h
    y = (y + bonus.reshape(B, T, RW_W)) * g
    return y, S

def moe_ffn(h, w_router, b_router, w_gate_up, b_gate_up, w_down, b_down):
    T = h.shape[0]
    logits = h.astype(F32) @ w_router.astype(F32) + b_router.astype(F32)
    top_val, top_idx = lax.top_k(logits, TOP_K)
    gates = jax.nn.softmax(top_val, axis=-1)
    TK = T * TOP_K
    flat_e = top_idx.reshape(-1)
    order = jnp.argsort(flat_e)
    sorted_e = flat_e[order]
    counts = jnp.bincount(flat_e, length=N_EXPERTS)
    padded = ((counts + MOE_BLOCK - 1) // MOE_BLOCK) * MOE_BLOCK
    ends = jnp.cumsum(padded)
    pad_start = ends - padded
    start = jnp.cumsum(counts) - counts
    rank = jnp.arange(TK, dtype=jnp.int32) - start[sorted_e]
    dest = pad_start[sorted_e] + rank
    n_blocks = -(-TK // MOE_BLOCK) + N_EXPERTS
    n_rows = n_blocks * MOE_BLOCK
    token_of_row = jnp.full((n_rows,), T, dtype=jnp.int32).at[dest].set((order // TOP_K).astype(jnp.int32))
    gate_of_row = jnp.zeros((n_rows,), F32).at[dest].set(gates.reshape(-1)[order])
    block_start = jnp.arange(n_blocks, dtype=jnp.int32) * MOE_BLOCK
    block_expert = jnp.minimum(jnp.searchsorted(ends, block_start, side='right'), N_EXPERTS - 1)
    h_pad = jnp.concatenate([h, jnp.zeros((1, h.shape[1]), h.dtype)], axis=0)
    xb = h_pad[token_of_row].reshape(n_blocks, MOE_BLOCK, h.shape[1])

    def expert_block(args):
        xblk, e = args
        gu = xblk.astype(F32) @ w_gate_up[e].astype(F32) + b_gate_up[e].astype(F32)
        gate, up = gu[:, :D_FF], gu[:, D_FF:]
        gate = jnp.minimum(gate, SWIGLU_LIMIT)
        up = jnp.clip(up, -SWIGLU_LIMIT, SWIGLU_LIMIT)
        glu = gate * jax.nn.sigmoid(SWIGLU_ALPHA * gate)
        return ((up + 1.0) * glu) @ w_down[e].astype(F32) + b_down[e].astype(F32)

    yb = lax.map(expert_block, (xb, block_expert)).reshape(n_rows, -1)
    y = jax.ops.segment_sum(yb * gate_of_row[:, None], token_of_row, num_segments=T + 1)[:T]
    return y.astype(h.dtype)

def trunk(x, st_hg, st_rw, st_shift, norm_mix, w_in, lb_logits, hg_norm_w, rw_mu, rw_w0, rw_w2,
          rw_a0, rw_a2, rw_g2, rw_k_k, rw_k_a, rw_r_k, rw_lnx_w, rw_lnx_b, w_out, norm_ffn,
          w_router, b_router, w_gate_up, b_gate_up, w_down, b_down, norm_final):
    B, T, _ = x.shape
    lbs = jnp.cumsum(jax.nn.softmax(lb_logits.astype(F32), axis=0), axis=0)
    new_hg, new_rw, new_shift = [], [], []
    for l in range(DEPTH):
        h = rmsnorm(x, norm_mix[l])
        proj = h @ w_in[l]
        hq = HG_H * HG_DK
        hv = HG_H * HG_DV
        q = proj[..., :hq]
        f_pre = proj[..., hq:2 * hq]
        i_in = proj[..., 2 * hq:2 * hq + hv]
        g_in = proj[..., 2 * hq + hv:HG_COLS]
        o_hg, s_hg = hgrn2_mix(q, f_pre, i_in, g_in, lbs[l], st_hg[l], hg_norm_w[l])
        p_prev = st_shift[l] @ w_in[l][:, HG_COLS:]
        o_rw, s_rw = rwkv7_mix(proj[..., HG_COLS:], p_prev, st_rw[l], rw_mu[l], rw_w0[l], rw_w2[l],
                               rw_a0[l], rw_a2[l], rw_g2[l], rw_k_k[l], rw_k_a[l], rw_r_k[l],
                               rw_lnx_w[l], rw_lnx_b[l])
        mixed = jnp.concatenate([o_hg, o_rw], axis=-1).astype(x.dtype)
        x = x + mixed @ w_out[l]
        hf = rmsnorm(x, norm_ffn[l]).reshape(B * T, D_MODEL)
        x = x + moe_ffn(hf, w_router[l], b_router[l], w_gate_up[l], b_gate_up[l],
                        w_down[l], b_down[l]).reshape(B, T, D_MODEL)
        new_hg.append(s_hg.astype(st_hg.dtype))
        new_rw.append(s_rw.astype(st_rw.dtype))
        new_shift.append(h[:, -1, :].astype(st_shift.dtype))
    return rmsnorm(x, norm_final), jnp.stack(new_hg), jnp.stack(new_rw), jnp.stack(new_shift)

def setup_inputs(seed: int = 0) -> dict:
    key = jax.random.key(seed)
    keys = jax.random.split(key, 32)
    ks = iter([keys[j] for j in range(32)])

    def nrm(shape, s):
        return jax.random.normal(next(ks), shape, F32) * s

    L = DEPTH
    return {
        "x_prompt": nrm((BATCH, SEQ, D_MODEL), 1.0),
        "x_sample": nrm((DEC_BATCH, DEC_SEQ, D_MODEL), 1.0),
        "state_hgrn": nrm((L, DEC_BATCH, HG_H, HG_DK, HG_DV), 0.5),
        "state_rwkv": nrm((L, DEC_BATCH, RW_H, RW_N, RW_N), 0.2),
        "state_shift": nrm((L, DEC_BATCH, D_MODEL), 1.0),
        "norm_mix": 1.0 + nrm((L, D_MODEL), 0.05),
        "w_in": nrm((L, D_MODEL, HG_COLS + RW_COLS), D_MODEL ** -0.5),
        "lb_logits": nrm((L + 1, HG_H * HG_DK), 1.0),
        "hg_norm_w": 1.0 + nrm((L, HG_DV), 0.05),
        "rw_mu": jax.random.uniform(next(ks), (L, RW_COLS), F32, 0.0, 1.0),
        "rw_w0": nrm((L, RW_W), 0.5),
        "rw_w2": nrm((L, RW_DECAY_LORA, RW_W), 0.1),
        "rw_a0": nrm((L, RW_W), 0.1),
        "rw_a2": nrm((L, RW_A_LORA, RW_W), 0.1),
        "rw_g2": nrm((L, RW_G_LORA, RW_W), RW_G_LORA ** -0.5),
        "rw_k_k": 0.85 + nrm((L, RW_W), 0.05),
        "rw_k_a": 1.0 + nrm((L, RW_W), 0.05),
        "rw_r_k": nrm((L, RW_H, RW_N), 0.1),
        "rw_lnx_w": 1.0 + nrm((L, RW_W), 0.05),
        "rw_lnx_b": nrm((L, RW_W), 0.01),
        "w_out": nrm((L, MIX_W, D_MODEL), MIX_W ** -0.5),
        "norm_ffn": 1.0 + nrm((L, D_MODEL), 0.05),
        "w_router": nrm((L, D_MODEL, N_EXPERTS), D_MODEL ** -0.5),
        "b_router": nrm((L, N_EXPERTS), 0.01),
        "w_gate_up": nrm((L, N_EXPERTS, D_MODEL, 2 * D_FF), D_MODEL ** -0.5),
        "b_gate_up": nrm((L, N_EXPERTS, 2 * D_FF), 0.01),
        "w_down": nrm((L, N_EXPERTS, D_FF, D_MODEL), D_FF ** -0.5),
        "b_down": nrm((L, N_EXPERTS, D_MODEL), 0.01),
        "norm_final": 1.0 + nrm((D_MODEL,), 0.05),
    }

def reference(x_prompt, x_sample, state_hgrn, state_rwkv, state_shift, norm_mix, w_in, lb_logits,
              hg_norm_w, rw_mu, rw_w0, rw_w2, rw_a0, rw_a2, rw_g2, rw_k_k, rw_k_a, rw_r_k,
              rw_lnx_w, rw_lnx_b, w_out, norm_ffn, w_router, b_router, w_gate_up, b_gate_up,
              w_down, b_down, norm_final):
    Bp = x_prompt.shape[0]
    zero_hg = jnp.zeros((DEPTH, Bp, HG_H, HG_DK, HG_DV), state_hgrn.dtype)
    zero_rw = jnp.zeros((DEPTH, Bp, RW_H, RW_N, RW_N), state_rwkv.dtype)
    zero_shift = jnp.zeros((DEPTH, Bp, D_MODEL), state_shift.dtype)
    y_prompt, hgrn_prompt, rwkv_prompt, shift_prompt = trunk(
        x_prompt, zero_hg, zero_rw, zero_shift, norm_mix, w_in, lb_logits, hg_norm_w, rw_mu,
        rw_w0, rw_w2, rw_a0, rw_a2, rw_g2, rw_k_k, rw_k_a, rw_r_k, rw_lnx_w, rw_lnx_b, w_out,
        norm_ffn, w_router, b_router, w_gate_up, b_gate_up, w_down, b_down, norm_final)
    y_sample, hgrn_sample, rwkv_sample, shift_sample = trunk(
        x_sample, state_hgrn, state_rwkv, state_shift, norm_mix, w_in, lb_logits, hg_norm_w, rw_mu,
        rw_w0, rw_w2, rw_a0, rw_a2, rw_g2, rw_k_k, rw_k_a, rw_r_k, rw_lnx_w, rw_lnx_b, w_out,
        norm_ffn, w_router, b_router, w_gate_up, b_gate_up, w_down, b_down, norm_final)
    return (y_prompt, y_sample, hgrn_prompt, rwkv_prompt, shift_prompt,
            hgrn_sample, rwkv_sample, shift_sample)


_drawn_inputs = setup_inputs


def setup_inputs(seed=0):
    import zlib

    import numpy as np

    out = dict(_drawn_inputs(seed))
    spreads = {}
    factors = {'rw_k_k': 3.363, 'b_gate_up': 8.0, 'b_down': 8.0}
    for name, (base, spread) in spreads.items():
        noise = np.random.default_rng([zlib.crc32(name.encode()), seed]).standard_normal(out[name].shape)
        drawn = base * np.exp(spread * noise) if base else spread * noise
        out[name] = __import__('jax').numpy.asarray(drawn.astype(out[name].dtype))
    for name, factor in factors.items():
        out[name] = (out[name] * factor).astype(out[name].dtype)
    return out
```

```python
import math
from contextlib import ExitStack

import concourse.bass as bass
from concourse import mybir

P = 128
F32 = mybir.dt.float32
I32 = mybir.dt.int32
U32 = mybir.dt.uint32
ALU = mybir.AluOpType
ACT = mybir.ActivationFunctionType
AX = mybir.AxisListType

DM = 1024
KT = DM // P
NP_, NS, TS = 256, 8, 8
NT = NP_ + NS * TS
NTP = NT + NS
TOFF, TN = [0, 128, 256], [128, 128, 64]
HGH, RWH, RN = 4, 8, 64
WIN = 3840
WORDER = [5, 7, 4, 6, 1, 0, 2, 3]
NE, TOPK, DFF = 32, 4, 1024
CAP = 64
NBLK = NT // CAP
CHUNK = 4096
EPS, GN_EPS = 1e-6, 64e-5
EDEC = math.exp(-0.5)
LIMIT, ALPHA = 7.0, 1.702
LEVELS = [1, 2, 4, 8, 16, 32, 64]
FAR = 4096.0

PR = {}
_n = 0
for _name, _k in (("lb0", 4), ("lb1", 4), ("mu", 14), ("w0", 4), ("a0", 4), ("kk", 4), ("ka", 4), ("rk", 4),
                  ("lnw", 4), ("lnb", 4), ("gnw", 1)):
    PR[_name] = (_n, _k)
    _n += _k
NPAR = _n


def proj_tiles():
    out = []
    for n, g in enumerate(WORDER):
        for i in range(2 if g == 7 else 4):
            out.append((4 * g + i, n, i))
    return out


PROJ = proj_tiles()
PPOS = {j: n for n, (j, _, _) in enumerate(PROJ)}


def psum_units():
    u = []

    def add(stage, n):
        k = sum(1 for s, _ in u if s == stage)
        u.extend((stage, k + i) for i in range(n))
    add("params", 1)
    add("hT", KT)
    add("proj", 14)
    add("wpre", 4)
    add("apre", 4)
    add("gpre", 4)
    add("proj", 8)
    add("kss", 1)
    add("proj", 4)
    add("knb", 4)
    add("proj", 4)
    add("itok", 3)
    for i, h in enumerate(LEVELS):
        add("lvl", 3 if h <= 4 else 2)
    add("lvl", 3)
    add("kstok", 3)
    add("hs1", 1)
    add("ho", 3)
    add("hs2", 1)
    add("hsend", 8)
    add("hvar", 1)
    add("hvarb", 4)
    add("bonus", 4)
    add("s0t", 4)
    add("vtok", 3)
    add("btok", 3)
    add("ktok", 3)
    for s in ("gM", "gN", "gK", "gRb", "gRk"):
        add(s, 6)
    for h in LEVELS[1:]:
        n = 6 if h <= 4 else 4
        add("mZ", n)
        add("mW", n)
        if h < 64:
            add("mT", n)
    add("rst", 2)
    for tile in range(3):
        add("R", 2)
        add("U", 2)
        add("Y", 2)
        if tile < 2:
            add("S", 2)
    add("send", 4)
    add("pst", 1)
    add("sout", 4)
    add("mean", 4)
    add("var", 1)
    add("varb", 4)
    add("xo", 6)
    add("bias", 2)
    add("h2T", KT)
    add("logit", 1)
    add("rank", 1)
    return u


UNITS = psum_units()
UPOS = {k: n for n, k in enumerate(UNITS)}


def build(nc, A, O):
    ctx = ExitStack()
    with ctx:
        def sb(name, shape, dt=F32):
            return ctx.enter_context(nc.sbuf_tensor(name, shape, dt))

        sems = {}

        def S(name):
            if name not in sems:
                sems[name] = ctx.enter_context(nc.semaphore(name))
            return sems[name]

        ring = sb("ring", [P, 6 * CHUNK])

        def slot(i):
            return ring[:, i * CHUNK:(i + 1) * CHUNK]
        OV = 2 * CHUNK

        def over(at, n):
            return ring[:, OV + at:OV + at + n]
        W5 = HGH * NT
        mix = sb("mix", [P, 13 * W5])

        def marr(i):
            return mix[:, i * W5:(i + 1) * W5].rearrange("p (j t) -> p j t", t=NT)
        hq, hf, hk, hi, hg = (marr(i) for i in range(5))
        rr, rk, rv, rg, rs, ra, rkk, rbon = (marr(i) for i in range(5, 13))
        hx = sb("hx", [P, 3 * DM])
        h = hx[:, :].rearrange("p (a d) -> p a d", d=DM)
        tA = hx[:, 0:W5].rearrange("p (j t) -> p j t", t=NT)
        tB = hx[:, W5:2 * W5].rearrange("p (j t) -> p j t", t=NT)
        hTb = sb("hTb", [P, KT * NTP])
        hT = hTb[:, :].rearrange("p (c t) -> p c t", t=NTP)
        ident = sb("ident", [P, P])
        ones = sb("ones", [P, P])
        blk = sb("blk", [P, P])
        blkm = sb("blkm", [P, P])
        mT = sb("mT", [P, len(LEVELS), P])
        mM = sb("mM", [P, P])
        strict = sb("strict", [P, P])
        incl = sb("incl", [P, P])
        strict8 = sb("strict8", [64, 64])
        incl8 = sb("incl8", [64, 64])
        seqm = sb("seqm", [64, NS])
        reset = rbon[:, 0, :]
        iota = sb("iota", [P, (NBLK + 2) * CAP])
        epst = sb("epst", [P, 2])
        gain = hTb[:, 0:DM]
        prow = hTb[:, 2 * DM:2 * DM + P]
        par = sb("par", [P, NPAR])
        der = sb("der", [P, 12])
        raw = sb("raw", [P, 2, NTP])
        dif = hx[:, 2 * W5:2 * W5 + NT]
        lor = sb("lor", [P, 2, NT])
        iotai = lor[:, :, :].rearrange("p a t -> p (a t)")[:, 0:(NBLK + 2) * CAP].bitcast(I32)
        junk = hTb[:, DM:2 * DM]
        w2a2 = sb("w2a2", [P, NE * 16])
        bgu = w2a2
        g2w = sb("g2w", [P, 512])
        st = sb("st", [P, 16])
        nrm = sb("nrm", [P, 4, 24])
        cen = sb("cen", [P, 2, 4])
        pc = sb("pc", [P, 4, 10])
        ec = sb("ec", [P, 8])
        sp = sb("sp", [P, 256])
        pout = g2w[0:64, :]

        def pcol(name, i=0):
            a, _ = PR[name]
            return par[:, a + i:a + i + 1]
        banks = [ctx.enter_context(nc.psum_tensor(f"bank{i}", [P, 512], F32)) for i in range(8)]

        def U(stage, k):
            return UPOS[stage, k - 1] + 1

        def half_done(x):
            return (S("send_half"), x // 2 + 1) if x % 2 == 0 else (S("unit_filled"), U("send", x // 2 + 1))

        def bank(stage, i):
            return banks[UPOS[stage, i] % 8]

        suf = over(0, W5).rearrange("p (j t) -> p j t", t=NT)
        qp = over(W5, W5).rearrange("p (j t) -> p j t", t=NT)
        ks = over(2 * W5, W5).rearrange("p (j t) -> p j t", t=NT)
        at_ = over(3 * W5, W5)
        itok = over(4 * W5, 1536).rearrange("p (a d) -> p a d", d=512)
        kstok = over(4 * W5 + 1536, 1536).rearrange("p (a d) -> p a d", d=512)
        hs0 = over(4 * W5 + 3072, 4096).rearrange("p (b h v) -> p b h v", b=NS, h=HGH)
        hs = over(4 * W5 + 7168, 512).rearrange("p (h v) -> p h v", v=P)
        imask = over(4 * W5 + 7680, 2048).rearrange("p (n b v) -> p n b v", n=2, v=P)
        MW = 2560

        def mats(t):
            def unit(tile, p, part=None):
                n = TN[tile]
                o = 1024 * tile + p * 4 * n
                return t[0:n, o:o + 4 * n].rearrange("p (j t) -> p j t", t=n)
            return unit
        mM_, mT_, mW_, mZ_, mK_, mRb_ = (mats(over(i * MW, MW)) for i in range(6))
        mRk_ = mats(mix[:, W5:W5 + MW])
        vtok = hTb[:, 0:1536].rearrange("p (a d) -> p a d", d=512)
        s0raw = hTb[:, 0:2048].rearrange("p (b h k) -> p b h k", b=4, h=RWH)
        btok = hx[:, 0:1536].rearrange("p (a d) -> p a d", d=512)
        ktok = hx[:, 1536:3072].rearrange("p (a d) -> p a d", d=512)
        s0t = mix[:, 3 * W5:3 * W5 + 2048].rearrange("p (b j c v) -> p b j c v", b=4, j=4, c=2)
        uu = over(0, 1536).rearrange("p (a d) -> p a d", d=512)
        rR = over(3 * MW, 1536).rearrange("p (a d) -> p a d", d=512)
        um = over(MW, 1024).rearrange("p (n b v) -> p n b v", n=2, v=RN)
        vm = over(MW + 1024, 1024).rearrange("p (n b v) -> p n b v", n=2, v=RN)
        rst = over(3 * MW + 1536, 256).rearrange("p (j t) -> p j t", t=64)
        sout = over(4 * MW, 2048).rearrange("p (b j k) -> p b j k", b=4, j=4)
        yy = rk
        xres = h
        h2 = mix[:, 9 * W5:9 * W5 + 3072].rearrange("p (a d) -> p a d", d=DM)
        acc = mix[:, W5:W5 + KT * NT].rearrange("p (c t) -> p c t", t=NT)
        wr = sb("wr", [P, KT, NE])
        brow = sb("brow", [P, NE])
        lgt = sb("lgt", [P, 3, NE])
        top = sb("top", [P, 3, 8])
        topi = sb("topi", [P, 3, 8], U32)
        topf = sb("topf", [P, 3, 8])
        gat = sb("gat", [P, 3, 8])
        hot = sb("hot", [P, NE])
        msk = sb("msk", [P, 3, NE])
        gate = sb("gate", [P, 3, NE + 2])
        rnk = sb("rnk", [P, 3, NE + 2])
        flag = sb("flag", [P, 2])
        flagi = sb("flagi", [1, 1], I32)
        bdn = sb("bdn", [P, NE * 8])
        E0 = 3 * W5
        brows = mix[:, E0:E0 + 768].rearrange("p (a d) -> p a d", d=P)
        sel = mix[:, E0 + 768:E0 + 768 + 384].rearrange("p (a c) -> p a c", c=P)
        selg = mix[:, E0 + 1152:E0 + 1536].rearrange("p (a c) -> p a c", c=P)
        xgf = mix[:, E0 + 1536:E0 + 2560].rearrange("p (c s) -> p c s", s=P)
        h1 = mix[:, E0 + 2560:E0 + 3584].rearrange("p (n c s) -> p n c s", n=2, s=CAP)
        yt = mix[:, E0 + 3584:E0 + 4608].rearrange("p (c s) -> p c s", s=P)
        ytk = mix[:, E0 + 4608:E0 + 5632]
        scat = mix[:, E0 + 5632:E0 + 5952]
        gg = mix[:, E0 + 5952:E0 + 6464].rearrange("p (c s) -> p c s", s=CAP)
        sg = mix[:, E0 + 6464:E0 + 6976].rearrange("p (c s) -> p c s", s=CAP)
        upv = mix[:, E0 + 6976:E0 + 7488].rearrange("p (c s) -> p c s", s=CAP)
        assert E0 + 7488 <= 9 * W5
        yrow = ring[:, 0:3 * DM].rearrange("p (a d) -> p a d", d=DM)

        def bc(ap, n):
            return ap.unsqueeze(2).broadcast_to([ap.shape[0], ap.shape[1], n])

        def rep(ap, n):
            return ap.unsqueeze(1).broadcast_to([ap.shape[0], n, ap.shape[1]])

        def npair(h_):
            return NT if h_ <= 4 else NP_

        NPAIR = NE // 2

        block = ctx.enter_context(nc.Block())

        @block.sync
        def _(sync):
            def load(dst, src, name):
                sync.dma_start(dst, src).then_inc(S(name), 16)

            def params(name, src):
                a, k = PR[name]
                load(prow[a:a + k, :], src, "prow_in")
            xp, xs = A["x_prompt"], A["x_sample"]
            load(h[:, 0, :], xp[0, 0:P, :], "x_in")
            load(h[:, 1, :], xp[0, P:2 * P, :], "x_in")
            load(h[0:64, 2, :], xs.rearrange("b t d -> (b t) d"), "x_in")
            load(h[64:72, 2, :], A["state_shift"][0], "x_in")
            load(gain[:, :], A["norm_mix"].broadcast_to([P, DM]), "gain_in")
            params("lb0", A["lb_logits"][0:1, :].rearrange("a (h p) -> (a h) p", p=P))
            params("lb1", A["lb_logits"][1:2, :].rearrange("a (h p) -> (a h) p", p=P))
            for nm, src in (("mu", "rw_mu"), ("w0", "rw_w0"), ("a0", "rw_a0"), ("kk", "rw_k_k"), ("ka", "rw_k_a"),
                            ("lnw", "rw_lnx_w"), ("lnb", "rw_lnx_b")):
                params(nm, A[src].rearrange("a (h p) -> (a h) p", p=P))
            params("rk", A["rw_r_k"][0].rearrange("(j h) n -> j (h n)", h=2))
            params("gnw", A["hg_norm_w"])
            w_in = A["w_in"][0].rearrange("(c p) n -> p c n", p=P)
            for n, g in enumerate(WORDER):
                if n >= 6:
                    last = max(i for i, (_, m, _) in enumerate(PROJ) if m == n - 6)
                    sync.wait_ge(S("unit_filled"), U("proj", last + 1))
                w = 256 if g == 7 else 512
                load(slot(n % 6).rearrange("p (c n) -> p c n", c=KT)[:, :, 0:w], w_in[:, :, 512 * g:512 * g + w], f"ring{n % 6}")
                if n == 1:
                    load(w2a2[0:64, :], A["rw_w2"][0], "lora_in")
                    load(w2a2[64:128, :], A["rw_a2"][0], "lora_in")
                    load(g2w[:, :], A["rw_g2"][0], "lora_in")
            sync.wait_ge(S("unit_filled"), U("proj", PPOS[4 * WORDER[5] + 3] + 1))
            load(hs0, A["state_hgrn"][0].rearrange("b h k v -> k b h v"), "hs0_in")
            sync.wait_ge(S("unit_filled"), U("proj", 30))
            w_out = A["w_out"][0].rearrange("(c p) n -> p c n", p=P)
            for i in range(2):
                load(slot(i).rearrange("p (c n) -> p c n", n=DM), w_out[:, 4 * i:4 * i + 4, :], f"ring{i}")
            srw = A["state_rwkv"][0].rearrange("(b c) h v k -> c v b h k", c=2)
            for c in range(2):
                for q in range(4):
                    load(s0raw[64 * c:64 * c + 64, q], srw[c][:, q], "s0_in")
            load(wr[:, :, :], A["w_router"][0].rearrange("(c p) n -> p c n", p=P), "router_in")
            load(brow[:, :], A["b_router"].broadcast_to([P, NE]), "router_in")
            sync.wait_ge(S("unit_filled"), U("send", 4))
            load(h[:, 0, :], xp[0, 0:P, :], "xres_in")
            load(h[:, 1, :], xp[0, P:2 * P, :], "xres_in")
            load(h[0:64, 2, :], xs.rearrange("b t d -> (b t) d"), "xres_in")
            sync.wait_ge(S("send_ready"), 4)
            sync.wait_ge(S("unit_filled"), U("sout", 4))
            bg = A["b_gate_up"][0].rearrange("e (c p) -> (e c) p", p=P)
            bd = A["b_down"][0].rearrange("e (c p) -> (e c) p", p=P)
            load(brows[:, 0:4, :], bg.rearrange("(a q) p -> q a p", q=P), "brow_in")
            load(brows[:, 4:6, :], bd.rearrange("(a q) p -> q a p", q=P), "brow_in")
            load(gain[:, :], A["norm_ffn"].broadcast_to([P, DM]), "gain2_in")
            sync.wait_ge(S("unit_filled"), U("logit", 1))
            load(gain[:, :], A["norm_final"].rearrange("(a d) -> a d", a=1).broadcast_to([P, DM]), "gain3_in")

            wgu = A["w_gate_up"][0].rearrange("e (c p) n -> p e c n", p=P)
            wdn = A["w_down"][0].rearrange("e (c p) n -> p e c n", p=P)

            def expert(e, used, k):
                for i in range(6):
                    if used:
                        sync.wait_ge(S(f"wt{i}"), 16)
                        sync.wait_ge(S(f"used{i}"), k)
                    if i < 4:
                        src = wgu[:, e, 2 * i:2 * i + 2, :]
                        dst = slot(i).rearrange("p (c n) -> p c n", n=2 * DFF)
                    else:
                        src = wdn[:, e, 4 * (i - 4):4 * (i - 4) + 4, :]
                        dst = slot(i).rearrange("p (c n) -> p c n", n=DM)
                    load(dst, src, f"wt{i}")
            for i in (2, 3, 4, 5, 0, 1):
                if i == 2:
                    sync.wait_ge(S("mixer_done"), 1)
                    sync.wait_ge(S("rwkv_out"), 128)
                if i == 0:
                    sync.wait_ge(S("unit_filled"), U("xo", 6))
                if i < 4:
                    load(slot(i).rearrange("p (c n) -> p c n", n=2 * DFF), wgu[:, 0, 2 * i:2 * i + 2, :], f"wt{i}")
                else:
                    load(slot(i).rearrange("p (c n) -> p c n", n=DM), wdn[:, 0, 4 * (i - 4):4 * (i - 4) + 4, :], f"wt{i}")
            with sync.Fori(1, NE) as e:
                expert(e, True, e)
            sync.wait_ge(S("flag_ready"), 1)
            over_ = sync.value_load(flagi[0:1, 0:1], min_val=0, max_val=1)
            with sync.If(over_ > 0):
                with sync.Fori(NE, NE * NBLK) as n:
                    expert(n & (NE - 1), True, n)
            sync.nop()
            sync.wait_ge(S("y_done"), 3)
            for tile in range(3):
                dst = (O[0][0, P * tile:P * tile + P, :] if tile < 2 else O[1].rearrange("b t d -> (b t) d"))
                sync.dma_start(dst, yrow[0:TN[tile], tile, :]).then_inc(S("y_out"), 16)
            sync.wait_ge(S("y_out"), 48)

        @block.gpsimd
        def _(pool):
            n = [0]

            def link(ins):
                n[0] += 1
                ins.then_inc(S("pool_chain"), 1)
                pool.wait_ge(S("pool_chain"), n[0])
            g = nc.gpsimd
            link(g.memset(ones[:, :], 1.0))
            link(g.memset(ident[:, :], 0.0))
            link(g.memset(blk[:, :], 0.0))
            link(g.memset(blkm[:, :], 0.0))
            link(g.memset(mT[:, :, :], 0.0))
            link(g.memset(mM[:, :], 0.0))
            link(g.memset(reset[:, :], 1.0))
            link(g.memset(epst[:, 0:1], EPS))
            link(g.memset(epst[:, 1:2], GN_EPS))
            link(g.memset(st[:, :], 1.0))
            link(g.memset(blk[0:64, 0:64], 1.0))
            link(g.memset(blk[64:128, 64:128], 1.0))
            link(g.memset(blkm[0:64, 0:64], 1.0 / RN))
            link(g.memset(blkm[64:128, 64:128], 1.0 / RN))
            link(g.memset(reset[:, 0:P + 1:P], 0.0))
            link(g.memset(reset[:, NP_:NT:TS], 0.0))
            link(g.affine_select(out=ident[:, :], in_=ident[:, :], compare_op=ALU.not_equal, fill=1.0, base=0,
                                 pattern=[[-1, P]], channel_multiplier=1))
            g.memset(st[0:1, 15:16], 1.0).then_inc(S("ident_ready"), 1)

            def select(out, in_, pattern, base, ch):
                link(g.affine_select(out=out, in_=in_, compare_op=ALU.is_ge, fill=0.0, base=base, pattern=pattern,
                                     channel_multiplier=ch))
            for i, hh in enumerate(LEVELS):
                nb = P // (2 * hh)
                v = mT[:, i, :].rearrange("p (b a c) -> p b a c", a=2, c=hh)[:, :, 1, :]
                o = ones[:, 0:nb * hh].rearrange("p (b c) -> p b c", c=hh)
                select(v, o, [[-2 * hh, nb], [0, hh]], 0, 1)
                select(v, v, [[2 * hh, nb], [0, hh]], hh - 1, -1)
            v = mM[:, :].rearrange("p (b a) -> p b a", a=2)[:, :, 0:1]
            o = ones[:, 0:64].rearrange("p (b c) -> p b c", c=1)
            select(v, o, [[-2, 64], [0, 1]], -1, 1)
            select(v, v, [[2, 64], [0, 1]], 1, -1)
            select(strict[:, :], ones[:, :], [[1, P]], -1, -1)
            select(incl[:, :], ones[:, :], [[1, P]], 0, -1)
            s8 = strict8[:, :].rearrange("p (b c) -> p b c", c=TS)
            i8 = incl8[:, :].rearrange("p (b c) -> p b c", c=TS)
            o8 = ones[0:64, 0:64].rearrange("p (b c) -> p b c", c=TS)
            select(s8, o8, [[-TS, NS], [0, TS]], 0, 1)
            select(s8, s8, [[TS, NS], [1, TS]], -1, -1)
            select(i8, o8, [[-TS, NS], [0, TS]], 0, 1)
            select(i8, i8, [[TS, NS], [1, TS]], 0, -1)
            select(seqm[:, :], ones[0:64, 0:NS], [[-TS, NS]], 0, 1)
            select(seqm[:, :], seqm[:, :], [[TS, NS]], TS - 1, -1)
            link(g.iota(iotai[:, :], [[1, (NBLK + 2) * CAP]], base=0, channel_multiplier=0))
            g.tensor_copy(iota[:, :], iotai[:, :]).then_inc(S("consts_ready"), 1)

            pool.wait_ge(S("h_done"), 1)
            pool.dma_start(O[4][0], h[P - 1:P, 1, :]).then_inc(S("shift_out"), 16)
            for b in range(NS):
                pool.dma_start(O[7][0, b:b + 1, :], h[TS * b + TS - 1:TS * b + TS, 2, :]).then_inc(S("shift_out"), 16)

            pool.wait_ge(S("hk_ready"), 4)
            pool.wait_ge(S("unit_filled"), U("proj", PPOS[4 * WORDER[5] + 3] + 1))
            link(g.memset(suf[:, :, :], 1.0))
            pool.wait_ge(S("at_zero"), 1)
            for i, hh in enumerate(LEVELS):
                if i:
                    pool.wait_ge(S("unit_filled"), U("lvl", sum(3 if x <= 4 else 2 for x in LEVELS[:i])))
                    g.tensor_tensor(ks[:, :, :], hk[:, :, :], suf[:, :, :], ALU.mult).then_inc(S("ks_ready"), 1)
                    pool.wait_ge(S("ks_ready"), i)
                m = npair(hh)
                sv = suf[:, :, 0:m].rearrange("p j (b a c) -> p j b a c", a=2, c=hh)
                fv = hf[:, :, 0:m].rearrange("p j (b a c) -> p j b a c", a=2, c=hh)
                for j in range(4):
                    out = sv[:, j, :, 0, :]
                    tot = fv[:, j, :, 1, hh - 1:hh].broadcast_to([P, m // (2 * hh), hh])
                    last = g.tensor_tensor(out, out, tot, ALU.mult)
                    if j < 3:
                        link(last)
                last.then_inc(S("suf_ready"), 1)
                pool.wait_ge(S("suf_ready"), i + 1)
                pool.wait_ge(S("pre_ready"), i + 1)
            pool.wait_ge(S("unit_filled"), U("lvl", sum(3 if x <= 4 else 2 for x in LEVELS) + 3))
            g.tensor_tensor(ks[:, :, :], hk[:, :, :], suf[:, :, :], ALU.mult).then_inc(S("ks_ready"), 1)
            pool.wait_ge(S("ks_ready"), len(LEVELS))
            for j in range(HGH):
                pool.wait_ge(S("itok_ready"), 3)
                if j >= 2:
                    pool.wait_ge(S("unit_filled"), U("hsend", 2 * (j - 1)))
                g.tensor_tensor(imask[0:64, j % 2], rep(itok[0:64, 2, P * j:P * j + P], NS), bc(seqm[:, :], P),
                                ALU.mult).then_inc(S("imask_ready"), 1)
                pool.wait_ge(S("imask_ready"), j + 1)
            pool.wait_ge(S("hs2_ready"), 1)
            pool.dma_start(O[2][0, 0].rearrange("h k v -> k h v"), hs[:, :, :]).then_inc(S("hgrn_out"), 16)
            pool.wait_ge(S("hsend_ready"), 8)
            pool.dma_start(O[5][0].rearrange("b h k v -> k b h v"), hs0).then_inc(S("hgrn_out"), 16)
            pool.wait_ge(S("hgrn_out"), 32)
            for tile in range(3):
                for p in range(2):
                    tn = TN[tile]
                    pool.wait_ge(S("gM_ready"), 2 * tile + p + 1)
                    link(g.tensor_tensor(mT_(tile, p), mM_(tile, p), rep(mM[0:tn, 0:tn], 4), ALU.mult))
                    g.tensor_tensor(mT_(tile, p), mT_(tile, p), rep(ident[0:tn, 0:tn], 4), ALU.add)\
                        .then_inc(S("T1_ready"), 1)
                    pool.wait_ge(S("T1_ready"), 2 * tile + p + 1)
            pool.wait_ge(S("vtok_ready"), 3)
            pool.wait_ge(S("mW_ready"), 2 * 6 + 4 * 4)
            for x in range(RWH):
                if x >= 2:
                    pool.wait_ge(*half_done(x - 2))
                g.tensor_tensor(vm[0:64, x % 2], rep(vtok[0:64, 2, RN * x:RN * x + RN], NS), bc(seqm[:, :], RN),
                                ALU.mult).then_inc(S("vm_ready"), 1)
                pool.wait_ge(S("vm_ready"), x + 1)
            pool.wait_ge(S("pst_ready"), 1)
            pool.dma_start(O[3][0, 0].rearrange("h v k -> v h k"), pout[:, :].rearrange("p (h k) -> p h k", k=RN))\
                .then_inc(S("prompt_state_out"), 16)
            pool.wait_ge(S("sout_ready"), 4)
            ors = O[6][0].rearrange("(b c) h v k -> c v b h k", c=2)
            for c in range(2):
                for q in range(4):
                    pool.dma_start(ors[c][:, q], sout[64 * c:64 * c + 64, q].rearrange("p j (h k) -> p (j h) k", h=2))\
                        .then_inc(S("rwkv_out"), 16)
            pool.wait_ge(S("shift_out"), 16 * (NS + 1))
            pool.wait_ge(S("prompt_state_out"), 16)
            pool.wait_ge(S("rwkv_out"), 128)

        @block.tensor
        def _(pe):
            mm = nc.tensor.matmul

            def free(stage, i):
                n_ = UPOS[stage, i]
                if n_ >= 8:
                    s, k = UNITS[n_ - 8]
                    pe.wait_ge(S(f"{s}_ready"), k + 1)
                return banks[n_ % 8]

            def filled(ins, stage):
                ins.then_inc(S("unit_filled"), 1)

            pe.wait_ge(S("ident_ready"), 1)
            pe.wait_ge(S("prow_in"), 16 * 11)
            b = free("params", 0)
            filled(nc.tensor.transpose(b[:, 0:NPAR], prow[0:NPAR, :], ident[0:NPAR, 0:NPAR]), "params")
            pe.wait_ge(S("h_done"), 1)
            pe.wait_ge(S("x_in"), 64)
            for c in range(KT):
                b = free("hT", c)
                for tile in range(3):
                    tn = 72 if tile == 2 else P
                    last = nc.tensor.transpose(b[:, P * tile:P * tile + tn], h[0:tn, tile, P * c:P * c + P],
                                               ident[0:tn, 0:tn])
                filled(last, "hT")

            def proj(n0, n1):
                for n_ in range(n0, n1):
                    j, chunk, k = PROJ[n_]
                    pe.wait_ge(S(f"ring{chunk % 6}"), 16 * (chunk // 6 + 1))
                    pe.wait_ge(S("hT_ready"), KT)
                    b_ = free("proj", n_)
                    w = slot(chunk % 6).rearrange("p (c n) -> p c n", c=KT)
                    nn = NTP if j >= 16 else NT
                    for c in range(KT):
                        last_ = mm(b_[:, 0:nn], w[:, c, P * k:P * k + P], hT[:, c, 0:nn], start=(c == 0), stop=(c == KT - 1))
                    filled(last_, "proj")
            proj(0, 14)
            pe.wait_ge(S("lora_in"), 48)
            for j in range(4):
                pe.wait_ge(S("lora_act"), 1)
                b = free("wpre", j)
                filled(mm(b[:, 0:NT], w2a2[0:64, P * j:P * j + P], lor[0:64, 0, :], start=True, stop=True), "wpre")
            for j in range(4):
                b = free("apre", j)
                filled(mm(b[:, 0:NT], w2a2[64:128, P * j:P * j + P], lor[64:128, 0, :], start=True, stop=True), "apre")
            for j in range(4):
                pe.wait_ge(S("lora_act"), 2)
                b = free("gpre", j)
                filled(mm(b[:, 0:NT], g2w[:, P * j:P * j + P], lor[:, 1, :], start=True, stop=True), "gpre")
            proj(14, 22)

            def head_sums(stage, src, ready, count):
                pe.wait_ge(S(ready), count)
                b_ = free(stage, 0)
                for tile in range(3):
                    for j in range(4):
                        o = 8 * tile + 2 * j
                        last_ = mm(b_[0:TN[tile], o:o + 2], src[:, j, TOFF[tile]:TOFF[tile] + TN[tile]], blk[:, 0:65:64],
                                   start=True, stop=True)
                filled(last_, stage)

            def head_spread(stage, col, ready):
                pe.wait_ge(S(ready), 1)
                for j in range(4):
                    b_ = free(stage, j)
                    for tile in range(3):
                        tn = TN[tile]
                        for p_ in range(2):
                            src = nrm[0:tn, col, 8 * tile + 2 * j + p_:8 * tile + 2 * j + p_ + 1].broadcast_to([tn, RN])
                            last_ = mm(b_[64 * p_:64 * p_ + 64, TOFF[tile]:TOFF[tile] + tn], src, ident[0:tn, 0:tn],
                                       start=True, stop=True)
                    filled(last_, stage)
            head_sums("kss", tB, "ksq", 4)
            proj(22, 26)
            head_spread("knb", 1, "kinv_ready")
            proj(26, 30)
            for tile in range(3):
                b = free("itok", tile)
                for j in range(4):
                    last = nc.tensor.transpose(b[0:TN[tile], P * j:P * j + P], hi[:, j, TOFF[tile]:TOFF[tile] + TN[tile]],
                                               ident[:, :])
                filled(last, "itok")
            at = 0
            for i, hh in enumerate(LEVELS + [0]):
                if hh:
                    pe.wait_ge(S("qp_ready"), i + 1)
                    if i:
                        pe.wait_ge(S("ks_ready"), i)
                for tile in range(3 if hh <= 4 else 2):
                    tn, to = TN[tile], TOFF[tile]
                    b = free("lvl", at)
                    kk_ = ks if i and hh else hk
                    qq = qp if hh else hq
                    for j in range(4):
                        last = mm(b[0:tn, tn * j:tn * j + tn], kk_[:, j, to:to + tn], qq[:, j, to:to + tn], start=True, stop=True)
                    filled(last, "lvl")
                    at += 1
            pe.wait_ge(S("ks_ready"), len(LEVELS))
            for tile in range(3):
                b = free("kstok", tile)
                for j in range(4):
                    last = nc.tensor.transpose(b[0:TN[tile], P * j:P * j + P], ks[:, j, TOFF[tile]:TOFF[tile] + TN[tile]],
                                               ident[:, :])
                filled(last, "kstok")

            def at_tile(tile):
                tn = TN[tile]
                return at_[0:tn, 512 * tile:512 * tile + 4 * tn].rearrange("p (j t) -> p j t", t=tn)

            def hstate(stage, tile):
                b_ = free(stage, 0)
                for j in range(4):
                    last_ = mm(b_[:, P * j:P * j + P], kstok[:, tile, P * j:P * j + P], itok[:, tile, P * j:P * j + P],
                               start=True, stop=True)
                filled(last_, stage)
            pe.wait_ge(S("kstok_ready"), 3)
            pe.wait_ge(S("itok_ready"), 3)
            hstate("hs1", 0)
            pe.wait_ge(S("at_ready"), 1)
            pe.wait_ge(S("qp_ready"), 8)
            for tile in range(3):
                tn, to = TN[tile], TOFF[tile]
                b = free("ho", tile)
                if tile == 1:
                    pe.wait_ge(S("hs1_ready"), 1)
                if tile == 2:
                    pe.wait_ge(S("hs0_in"), 16)
                for j in range(4):
                    o = b[:, tn * j:tn * j + tn]
                    last = mm(o, itok[0:tn, tile, P * j:P * j + P], at_tile(tile)[:, j, :], start=True, stop=(tile == 0),
                              skip_group_check=True)
                    if tile == 1:
                        last = mm(o, hs[:, j, :], qp[:, j, to:to + tn], start=False, stop=True, skip_group_check=True)
                    if tile == 2:
                        for q in range(NS):
                            last = mm(o[:, TS * q:TS * q + TS], hs0[:, q, j, :], qp[:, j, to + TS * q:to + TS * q + TS],
                                      start=False, stop=(q == NS - 1), skip_group_check=True)
                filled(last, "ho")
            hstate("hs2", 1)
            for j in range(HGH):
                pe.wait_ge(S("imask_ready"), j + 1)
                for half in range(2):
                    b = free("hsend", 2 * j + half)
                    filled(mm(b[:, :], kstok[0:64, 2, P * j:P * j + P],
                              imask[0:64, j % 2, 4 * half:4 * half + 4, :].rearrange("p b v -> p (b v)"),
                              start=True, stop=True), "hsend")
            pe.wait_ge(S("osq"), 1)
            b = free("hvar", 0)
            for tile in range(3):
                for j in range(4):
                    last = mm(b[0:TN[tile], 4 * tile + j:4 * tile + j + 1], hi[:, j, TOFF[tile]:TOFF[tile] + TN[tile]],
                              ones[:, 0:1], start=True, stop=True)
            filled(last, "hvar")
            pe.wait_ge(S("oinv_ready"), 1)
            for j in range(4):
                b = free("hvarb", j)
                for tile in range(3):
                    tn = TN[tile]
                    last = nc.tensor.transpose(b[:, TOFF[tile]:TOFF[tile] + tn],
                                               nrm[0:tn, 2, 4 * tile + j:4 * tile + j + 1].broadcast_to([tn, P]),
                                               ident[0:tn, 0:tn])
                filled(last, "hvarb")
            pe.wait_ge(S("rbon_in"), 4)
            for j in range(4):
                b = free("bonus", j)
                filled(mm(b[:, 0:NT], blk[:, :], rbon[:, j, :], start=True, stop=True), "bonus")
            pe.wait_ge(S("s0_in"), 128)
            for q in range(4):
                b = free("s0t", q)
                for j in range(4):
                    last = nc.tensor.transpose(b[:, P * j:P * j + P],
                                               s0raw[:, q, 2 * j:2 * j + 2, :].rearrange("p h k -> p (h k)"), ident[:, :])
                filled(last, "s0t")

            def tokens(stage, src):
                for tile_ in range(3):
                    tn_, b_ = TN[tile_], free(stage, tile_)
                    for j_ in range(4):
                        last_ = nc.tensor.transpose(b_[0:tn_, P * j_:P * j_ + P], src[:, j_, TOFF[tile_]:TOFF[tile_] + tn_],
                                                    ident[:, :])
                    filled(last_, stage)
            pe.wait_ge(S("rw_ready"), 1)
            tokens("vtok", rv)
            tokens("btok", ra)
            tokens("ktok", rk)

            def gram(stage, lhs, rhs):
                for tile_ in range(3):
                    tn_, to_ = TN[tile_], TOFF[tile_]
                    for p_ in range(2):
                        b_ = free(stage, 2 * tile_ + p_)
                        rows = slice(64 * p_, 64 * p_ + 64)
                        for j_ in range(4):
                            last_ = mm(b_[0:tn_, tn_ * j_:tn_ * j_ + tn_], lhs[rows, j_, to_:to_ + tn_],
                                       rhs[rows, j_, to_:to_ + tn_], start=True, stop=True)
                        filled(last_, stage)
            gram("gM", rkk, ra)
            gram("gN", ra, rkk)
            gram("gK", rk, rkk)
            gram("gRb", ra, rr)
            gram("gRk", rk, rr)
            done = {"mZ": 0, "mW": 0, "mT": 0}
            for i, hh in enumerate(LEVELS):
                if hh == 1:
                    continue
                units = [(tile, p) for tile in range(3 if hh <= 4 else 2) for p in range(2)]
                for stage, lhs, rhs in (("mZ", mM_, mW_), ("mW", mT_, mZ_), ("mT", mZ_, mT_)):
                    if stage == "mT" and hh == 64:
                        continue
                    for x, (tile, p) in enumerate(units):
                        tn, k = TN[tile], done[stage]
                        if stage == "mZ":
                            pe.wait_ge(S("gM_ready"), 6)
                            if hh == 2:
                                pe.wait_ge(S("gN_ready"), x + 1)
                            else:
                                pe.wait_ge(S("mW_ready"), done["mW"] - (6 if hh <= 8 else 4) + x + 1)
                        else:
                            pe.wait_ge(S("mZ_ready"), done["mZ"] - len(units) + x + 1)
                            if hh == 2:
                                pe.wait_ge(S("T1_ready"), x + 1)
                            elif stage == "mW":
                                pe.wait_ge(S("mT_ready"), done["mT"] - (6 if hh <= 8 else 4) + x + 1)
                        b = free(stage, k)
                        for j in range(4):
                            last = mm(b[0:tn, tn * j:tn * j + tn], lhs(tile, p)[:, j, :], rhs(tile, p)[:, j, :],
                                      start=True, stop=True)
                        filled(last, stage)
                        done[stage] += 1
            pe.wait_ge(S("s0t_ready"), 4)
            for p in range(2):
                b = free("rst", p)
                rows = slice(64 * p, 64 * p + 64)
                for j in range(4):
                    for q in range(NS):
                        o = 64 * j + TS * q
                        last = mm(b[rows, o:o + TS], s0t[rows, q // 2, j, q % 2, :], rkk[rows, j, NP_ + TS * q:NP_ + TS * q + TS],
                                  start=True, stop=True)
                filled(last, "rst")
            pe.wait_ge(S("mW_ready"), 28)
            pe.wait_ge(S("vtok_ready"), 3)
            pe.wait_ge(S("btok_ready"), 3)
            pe.wait_ge(S("ktok_ready"), 3)
            for tile in range(3):
                tn, to = TN[tile], TOFF[tile]
                if tile == 1:
                    pe.wait_ge(S("S_ready"), 2)
                if tile == 2:
                    pe.wait_ge(S("rst_ready"), 2)
                for p in range(2):
                    rows = slice(64 * p, 64 * p + 64)
                    b = free("R", 2 * tile + p)
                    for j in range(4):
                        hd = slice(P * j + 64 * p, P * j + 64 * p + 64)
                        o = b[0:tn, 64 * j:64 * j + 64]
                        last = mm(o, mK_(tile, p)[:, j, :], vtok[0:tn, tile, hd], start=True, stop=(tile == 0))
                        if tile == 1:
                            last = mm(o, rkk[rows, j, to:to + tn], sp[rows, 64 * j:64 * j + 64], start=False, stop=True)
                        if tile == 2:
                            last = mm(o, rst[:, j, :], ident[:, rows], start=False, stop=True)
                    filled(last, "R")
                for p in range(2):
                    pe.wait_ge(S("R_ready"), 2 * tile + p + 1)
                    b = free("U", 2 * tile + p)
                    for j in range(4):
                        hd = slice(P * j + 64 * p, P * j + 64 * p + 64)
                        last = mm(b[0:tn, 64 * j:64 * j + 64], mW_(tile, p)[:, j, :], rR[0:tn, tile, hd], start=True, stop=True)
                    filled(last, "U")
                for p in range(2):
                    pe.wait_ge(S("U_ready"), 2 * tile + p + 1)
                    rows = slice(64 * p, 64 * p + 64)
                    b = free("Y", 2 * tile + p)
                    for j in range(4):
                        hd = slice(P * j + 64 * p, P * j + 64 * p + 64)
                        o = b[rows, tn * j:tn * j + tn]
                        mm(o, uu[0:tn, tile, hd], mRb_(tile, p)[:, j, :], start=(tile < 2 or j == 0), stop=False,
                           skip_group_check=True)
                        last = mm(o, vtok[0:tn, tile, hd], mRk_(tile, p)[:, j, :], start=False, stop=(tile == 0),
                                  skip_group_check=True)
                        if tile == 1:
                            last = mm(o, sp[rows, 64 * j:64 * j + 64], rr[rows, j, to:to + tn], start=False, stop=True,
                                      skip_group_check=True)
                    if tile == 2:
                        last.then_inc(S("y_half"), 1)
                        pe.wait_ge(S("y_half"), p + 1)
                        for j in range(4):
                            o = b[rows, tn * j:tn * j + tn]
                            for q in range(NS):
                                t0 = NP_ + TS * q
                                last = mm(o[:, TS * q:TS * q + TS], s0t[rows, q // 2, j, q % 2, :], rr[rows, j, t0:t0 + TS],
                                          start=False, stop=(q == NS - 1), skip_group_check=True)
                    filled(last, "Y")
                if tile < 2:
                    for p in range(2):
                        rows = slice(64 * p, 64 * p + 64)
                        b = free("S", 2 * tile + p)
                        for j in range(4):
                            hd = slice(P * j + 64 * p, P * j + 64 * p + 64)
                            o = b[rows, 64 * j:64 * j + 64]
                            mm(o, btok[:, tile, hd], uu[:, tile, hd], start=True, stop=False)
                            last = mm(o, ktok[:, tile, hd], vtok[:, tile, hd], start=False, stop=True)
                        filled(last, "S")
            for j in range(4):
                b = free("send", j)
                for p in range(2):
                    x = 2 * j + p
                    hd = slice(P * j + 64 * p, P * j + 64 * p + 64)
                    pe.wait_ge(S("um_ready"), x + 1)
                    pe.wait_ge(S("vm_ready"), x + 1)
                    o = b[64 * p:64 * p + 64, :]
                    mm(o, btok[0:64, 2, hd], um[0:64, x % 2].rearrange("p b v -> p (b v)"), start=True, stop=False)
                    last = mm(o, ktok[0:64, 2, hd], vm[0:64, x % 2].rearrange("p b v -> p (b v)"), start=False, stop=True)
                    if p == 0:
                        last.then_inc(S("send_half"), 1)
                filled(last, "send")
            pe.wait_ge(S("S_ready"), 4)
            b = free("pst", 0)
            for j in range(4):
                last = nc.tensor.transpose(b[0:64, P * j:P * j + P], sp[:, 64 * j:64 * j + 64], ident[:, :])
            filled(last, "pst")
            pe.wait_ge(S("send_ready"), 4)
            for q in range(4):
                b = free("sout", q)
                for j in range(4):
                    last = nc.tensor.transpose(b[:, P * j:P * j + P], s0t[:, q, j].rearrange("p c v -> p (c v)"), ident[:, :])
                filled(last, "sout")
            pe.wait_ge(S("Y_ready"), 6)
            for j in range(4):
                b = free("mean", j)
                filled(mm(b[:, 0:NT], blkm[:, :], yy[:, j, :], start=True, stop=True), "mean")
            head_sums("var", ra, "ysq", 4)
            head_spread("varb", 3, "yinv_ready")
            pe.wait_ge(S("mixer_done"), 1)
            pe.wait_ge(S("mix_hg"), 1)
            for i in range(2):
                pe.wait_ge(S(f"ring{i}"), 48)
            for tile in range(3):
                for half in range(2):
                    b = free("xo", 2 * tile + half)
                    tn, to = TN[tile], TOFF[tile]
                    for c in range(KT):
                        lhs = (hq if c < 4 else yy)[:, c % 4, to:to + tn]
                        o = (c % 4) * DM + 512 * half
                        last = mm(b[0:tn, :], lhs, slot(c // 4)[:, o:o + 512], start=(c == 0), stop=(c == KT - 1))
                    filled(last, "xo")
            pe.wait_ge(S("brow_in"), 32)
            for i, k in enumerate((4, 2)):
                b = free("bias", i)
                for a in range(k):
                    last = nc.tensor.transpose(b[:, P * a:P * a + P], brows[:, 4 * i + a, :], ident[:, :])
                filled(last, "bias")
            pe.wait_ge(S("h_done"), 2)
            for c in range(KT):
                b = free("h2T", c)
                for tile in range(3):
                    tn = TN[tile]
                    last = nc.tensor.transpose(b[:, P * tile:P * tile + tn], h2[0:tn, tile, P * c:P * c + P], ident[0:tn, 0:tn])
                filled(last, "h2T")
            pe.wait_ge(S("h2T_ready"), KT)
            pe.wait_ge(S("router_in"), 32)
            b = free("logit", 0)
            for tile in range(3):
                for c in range(KT):
                    last = mm(b[0:TN[tile], NE * tile:NE * tile + NE], hT[:, c, TOFF[tile]:TOFF[tile] + TN[tile]], wr[:, c, :],
                              start=(c == 0), stop=(c == KT - 1))
            filled(last, "logit")
            pe.wait_ge(S("msk_ready"), 3)
            b = free("rank", 0)
            for tile in range(3):
                tn = TN[tile]
                for e_ in range(tile):
                    mm(b[0:tn, NE * tile:NE * tile + NE], ones[:, 0:tn], msk[:, e_, :], start=(e_ == 0), stop=False)
                mm(b[0:tn, NE * tile:NE * tile + NE], strict[0:tn, 0:tn], msk[0:tn, tile, :], start=(tile == 0), stop=True)
            for tile in range(3):
                tn = TN[tile]
                last = mm(b[0:1, 96:96 + NE], ones[0:tn, 0:1], msk[0:tn, tile, :], start=(tile == 0), stop=(tile == 2))
            filled(last, "rank")

            bG, bU, bX, bS, bD, bY = banks[0], banks[1], banks[2:4], banks[4], banks[5], banks[6:8]

            def gather(k, half):
                pe.wait_ge(S("sel_ready"), k + 1)
                for c in range(4 * half, 4 * half + 4):
                    for tile_ in range(3):
                        tn_ = TN[tile_]
                        last_ = mm(bX[c // 4][:, P * (c % 4):P * (c % 4) + P], h2[0:tn_, tile_, P * c:P * c + P],
                                   sel[0:tn_, tile_, :], start=(tile_ == 0), stop=(tile_ == 2))
                last_.then_inc(S("gathered"), 1)

            def up(k, ab, before):
                e = k * 2 + ab
                pe.wait_ge(S("xg_ready"), k + 1)
                pe.wait_ge(S("gu_read"), 2 * e)
                for c in range(KT):
                    if c % 2 == 0:
                        pe.wait_ge(S(f"wt{c // 2}"), (e + 1) * 16)
                    w = slot(c // 2)
                    for j in range(16):
                        o = (c % 2) * 2 * DFF + P * j
                        last_ = mm((bG, bU)[j // 8][:, CAP * (j % 8):CAP * (j % 8) + CAP], w[:, o:o + P],
                                   xgv(c, ab),
                                   start=(c == 0 and j % 8 == 0), stop=(c == KT - 1), skip_group_check=True)
                    if c % 2 == 1:
                        last_.then_inc(S(f"used{c // 2}"), 1)
                    if before and c == 1:
                        turn(k - 1)
                    if before and 3 <= c <= 6:
                        scatter(k - 1, 2 * (c - 3))

            def down(k, ab):
                e = k * 2 + ab
                pe.wait_ge(S("y_read"), e)
                for c in range(KT):
                    if c % 4 == 0:
                        pe.wait_ge(S("h1_ready"), 2 * e + c // 4 + 1)
                        pe.wait_ge(S(f"wt{4 + c // 4}"), (e + 1) * 16)
                    for d in range(KT):
                        o = (c % 4) * DM + P * d
                        last_ = mm(bD[:, CAP * d:CAP * d + CAP], slot(4 + c // 4)[:, o:o + P], h1[:, ab, c, :],
                                   start=(c == 0 and d == 0), stop=(c == KT - 1), skip_group_check=True)
                    if c % 4 == 3:
                        last_.then_inc(S(f"used{4 + c // 4}"), 1)

            def turn(k):
                pe.wait_ge(S("selg_ready"), k + 1)
                pe.wait_ge(S("scat_ready"), k)
                for tile_ in range(3):
                    tn_ = TN[tile_]
                    last_ = nc.tensor.transpose(bS[:, TOFF[tile_]:TOFF[tile_] + tn_], selg[0:tn_, tile_, :], ident[0:tn_, 0:tn_])
                last_.then_inc(S("selg_turned"), 1)
                pe.wait_ge(S("y_read"), 2 * k + 2)
                pe.wait_ge(S("acc_added"), 8 * k)
                for c in range(KT):
                    last_ = nc.tensor.transpose(bY[c // 4][:, P * (c % 4):P * (c % 4) + P], yt[:, c, :], ident[:, :])
                last_.then_inc(S("y_turned"), 1)

            def scatter(k, c0):
                pe.wait_ge(S("ytk_ready"), k + 1)
                for c in (c0, c0 + 1):
                    if c >= 2:
                        pe.wait_ge(S("acc_added"), 8 * k + c - 1)
                    mm(bY[c % 2][:, 0:NT], ytk[:, P * c:P * c + P], scat[:, :], start=True, stop=True)\
                        .then_inc(S("scattered"), 1)

            def pair(k, before):
                up(k, 0, before)
                gather(k + 1, 0)
                down(k, 0)
                up(k, 1, False)
                gather(k + 1, 1)
                down(k, 1)

            def finish(k):
                turn(k)
                for c0 in range(0, KT, 2):
                    scatter(k, c0)

            def xgv(c, ab):
                return xgf[:, c, CAP * ab:CAP * ab + CAP]
            for s, k in (("h2T", KT), ("logit", 1), ("rank", 1), ("bias", 2)):
                pe.wait_ge(S(f"{s}_ready"), k)
            gather(0, 0)
            gather(0, 1)
            pair(0, False)
            with pe.Fori(1, NPAIR) as k:
                pair(k, True)
            finish(NPAIR - 1)
            pe.wait_ge(S("flag_ready"), 1)
            over_ = pe.value_load(flagi[0:1, 0:1], min_val=0, max_val=1)
            with pe.If(over_ > 0):
                with pe.Fori(NPAIR, NPAIR * NBLK) as k:
                    pair(k, False)
                    finish(k)
            pe.nop()
            pe.wait_ge(S("acc_done"), 1)
            for tile in range(3):
                tn, to = TN[tile], TOFF[tile]
                for c in range(KT):
                    last = nc.tensor.transpose(banks[2 * tile + c // 4][0:tn, P * (c % 4):P * (c % 4) + P],
                                               acc[:, c, to:to + tn], ident[:, :])
                last.then_inc(S("acc_turned"), 1)

        @block.scalar
        def _(act):
            a = nc.scalar.activation
            cp = nc.scalar.copy

            def wait_filled(stage, i):
                act.wait_ge(S("unit_filled"), U(stage, i + 1))
                return bank(stage, i)

            def ready(ins, stage):
                ins.then_inc(S(f"{stage}_ready"), 1)

            def norms(k, src, rows=(P, P, 64)):
                for tile_ in range(3):
                    r_ = rows[tile_]
                    a(junk[0:r_, :], src[0:r_, tile_, :], ACT.Square, accum_out=st[0:r_, 3 * k + tile_:3 * k + tile_ + 1])\
                        .then_inc(S("ssq"), 1)
                    act.wait_ge(S("ssq"), 3 * k + tile_ + 1)
                a(st[:, 3 * k:3 * k + 3], st[:, 3 * k:3 * k + 3], ACT.Sqrt, scale=1.0 / DM, bias=epst[:, 0:1])\
                    .then_inc(S("rms"), 1)
            act.wait_ge(S("x_in"), 64)
            act.wait_ge(S("ident_ready"), 1)
            norms(0, h)
            act.wait_ge(S("par_ready"), 1)
            a(der[:, 0:4], der[:, 0:4], ACT.Sigmoid).then_inc(S("lb_ready"), 1)
            nraw = 0
            for n, (j, _, _) in enumerate(PROJ):
                b = wait_filled("proj", n)
                if 12 <= j < 16 or j < 4:
                    if n >= 2:
                        act.wait_ge(S("raw_used"), nraw - 1)
                    dst = hq if j < 4 else hg
                    a(dst[:, j % 4, :], b[:, 0:NT], ACT.Sigmoid)
                    ready(cp(raw[:, nraw % 2, 0:NT], b[:, 0:NT]), "proj")
                    nraw += 1
                elif j < 8:
                    ready(a(hf[:, j - 4, :], b[:, 0:NT], ACT.Sigmoid), "proj")
                elif j < 12:
                    ready(cp(hi[:, j - 8, :], b[:, 0:NT]), "proj")
                else:
                    if nraw >= 2:
                        act.wait_ge(S("raw_used"), nraw - 1)
                    ready(cp(raw[:, nraw % 2, :], b[:, 0:NTP]), "proj")
                    nraw += 1
                if j == 29:
                    act.wait_ge(S("lor_ready"), 2)
                    a(lor[0:64, 0, :], lor[0:64, 0, :], ACT.Tanh).then_inc(S("lora_act"), 1)
                    a(lor[:, 1, :], lor[:, 1, :], ACT.Sigmoid).then_inc(S("lora_act"), 1)
                if n == 13:
                    for j2 in range(4):
                        ready(a(rs[:, j2, :], wait_filled("wpre", j2)[:, 0:NT], ACT.Sigmoid, bias=pcol("w0", j2)), "wpre")
                    for j2 in range(4):
                        ready(a(ra[:, j2, :], wait_filled("apre", j2)[:, 0:NT], ACT.Sigmoid, bias=pcol("a0", j2)), "apre")
                    for j2 in range(4):
                        ready(cp(rg[:, j2, :], wait_filled("gpre", j2)[:, 0:NT]), "gpre")
                    act.wait_ge(S("mixed"), 14)
                    act.wait_ge(S("hT_ready"), KT)
                    for j2 in range(4):
                        a(tB[:, j2, :], rk[:, j2, :], ACT.Square, scale=pcol("kk", j2)).then_inc(S("ksq"), 1)
                if n == 21:
                    b = wait_filled("kss", 0)
                    a(nrm[:, 0, 0:16], b[:, 0:16], ACT.Sqrt)
                    ready(a(nrm[0:64, 0, 16:24], b[0:64, 16:24], ACT.Sqrt), "kss")
                if n == 25:
                    act.wait_ge(S("cen_ready"), 1)
                    a(ec[:, 0:4], cen[:, 1, :], ACT.Exp, scale=-EDEC)
                    act.wait_ge(S("gs_ready"), 1)
                    act.wait_ge(S("unit_filled"), U("kss", 1))
                    a(tB[:, :, :], tA[:, :, :], ACT.Exp, scale=EDEC).then_inc(S("e2_ready"), 1)
                    a(rs[:, :, :], rs[:, :, :], ACT.Exp, scale=-EDEC).then_inc(S("e3_ready"), 1)
                    act.wait_ge(S("e2_ready"), 1)
                    a(tA[:, :, :], tA[:, :, :], ACT.Exp, scale=-EDEC).then_inc(S("e1_ready"), 1)
            for tile in range(3):
                tn = TN[tile]
                ready(cp(itok[0:tn, tile, :], wait_filled("itok", tile)[0:tn, :]), "itok")
            for tile in range(3):
                tn = TN[tile]
                ready(cp(kstok[0:tn, tile, :], wait_filled("kstok", tile)[0:tn, :]), "kstok")
            ready(cp(hs[:, :, :], wait_filled("hs1", 0)[:, :].rearrange("p (h v) -> p h v", v=P)), "hs1")
            for tile in range(3):
                tn, to = TN[tile], TOFF[tile]
                src = wait_filled("ho", tile)[:, 0:4 * tn].rearrange("p (j t) -> p j t", t=tn)
                ready(cp(hq[:, :, to:to + tn], src), "ho")
            act.wait_ge(S("ho_ready"), 3)
            a(hi[:, :, :], hq[:, :, :], ACT.Square).then_inc(S("osq"), 1)
            b = wait_filled("hvar", 0)
            a(nrm[:, 2, 0:8], b[:, 0:8], ACT.Sqrt, scale=1.0 / P, bias=epst[:, 0:1])
            ready(a(nrm[0:64, 2, 8:12], b[0:64, 8:12], ACT.Sqrt, scale=1.0 / P, bias=epst[0:64, 0:1]), "hvar")
            act.wait_ge(S("mix_hg"), 1)
            for q in range(4):
                ready(cp(s0t[:, q].rearrange("p j c v -> p j (c v)"),
                         wait_filled("s0t", q)[:, :].rearrange("p (j x) -> p j x", j=4)), "s0t")
            for stage, dst in (("vtok", vtok), ("btok", btok), ("ktok", ktok)):
                for tile in range(3):
                    tn = TN[tile]
                    b = wait_filled(stage, tile)
                    if stage == "vtok":
                        act.wait_ge(S("unit_filled"), U("s0t", 4))
                    ready(cp(dst[0:tn, tile, :], b[0:tn, :]), stage)
            act.wait_ge(S("hgrn_out"), 32)
            act.wait_ge(S("mix_hg"), 1)
            for x in range(6):
                tn = TN[x // 2]
                ready(cp(mM_(x // 2, x % 2), wait_filled("gM", x)[0:tn, 0:4 * tn].rearrange("p (j t) -> p j t", t=tn)), "gM")
            act.wait_ge(S("unit_filled"), U("mZ", 28))
            act.wait_ge(S("unit_filled"), U("mW", 28))
            for p in range(2):
                b = wait_filled("rst", p)
                rows = slice(64 * p, 64 * p + 64)
                ready(cp(rst[rows, :, :], b[rows, 0:256].rearrange("p (j t) -> p j t", t=64)), "rst")
            for tile in range(3):
                tn, to = TN[tile], TOFF[tile]
                for stage, dst in (("R", rR), ("U", uu)):
                    for p in range(2):
                        b = wait_filled(stage, 2 * tile + p)
                        o = dst[0:tn, tile, :].rearrange("p (j c v) -> p j c v", c=2, v=RN)[:, :, p, :]
                        ready(cp(o, b[0:tn, 0:256].rearrange("p (j v) -> p j v", v=RN)), stage)
                for p in range(2):
                    rows = slice(64 * p, 64 * p + 64)
                    b = wait_filled("Y", 2 * tile + p)
                    ready(cp(yy[rows, :, to:to + tn], b[rows, 0:4 * tn].rearrange("p (j t) -> p j t", t=tn)), "Y")
            ready(cp(pout[:, :], wait_filled("pst", 0)[0:64, :]), "pst")
            for q in range(4):
                ready(cp(sout[:, q].rearrange("p j k -> p (j k)"), wait_filled("sout", q)[:, :]), "sout")
            act.wait_ge(S("yc_ready"), 4)
            for j in range(4):
                a(ra[:, j, :], yy[:, j, :], ACT.Square).then_inc(S("ysq"), 1)
            b = wait_filled("var", 0)
            a(nrm[:, 2, 0:16], b[:, 0:16], ACT.Sqrt, scale=1.0 / RN, bias=epst[:, 1:2])
            ready(a(nrm[0:64, 2, 16:24], b[0:64, 16:24], ACT.Sqrt, scale=1.0 / RN, bias=epst[0:64, 1:2]), "var")
            act.wait_ge(S("unit_filled"), U("bias", 1))
            ready(cp(bgu[:, :], bank("bias", 0)[:, :]), "bias")
            ready(cp(bdn[:, :], wait_filled("bias", 1)[:, 0:256]), "bias")
            act.wait_ge(S("xres_done"), 6)
            norms(1, h)
            act.wait_ge(S("top_ready"), 3)
            for tile in range(3):
                tn = TN[tile]
                a(gat[0:tn, tile, 0:4], gat[0:tn, tile, 0:4], ACT.Exp).then_inc(S("top_exp"), 1)

            def xg_out(k):
                for i in range(2):
                    act.wait_ge(S("gathered"), 2 * k + i + 1)
                    last_ = cp(xgf[:, 4 * i:4 * i + 4, :], banks[2 + i][:, :].rearrange("p (c s) -> p c s", s=P))
                last_.then_inc(S("xg_ready"), 1)

            def pair(k, before):
                if before:
                    finish(k - 1)
                for ab in range(2):
                    for i in range(2):
                        cs = slice(4 * i, 4 * i + 4)
                        act.wait_ge(S("gate_ready"), 2 * (k * 2 + ab) + i + 1)
                        a(sg[:, cs, :], gg[:, cs, :], ACT.Sigmoid, scale=ALPHA).then_inc(S("sig_ready"), 1)
                act.wait_ge(S("used3"), 2 * k + 2)
                xg_out(k + 1)

            def finish(k):
                act.wait_ge(S("selg_turned"), k + 1)
                act.wait_ge(S("scattered"), 8 * k)
                cp(scat[:, :], banks[4][:, 0:NT]).then_inc(S("scat_ready"), 1)
                act.wait_ge(S("y_turned"), k + 1)
                for i in range(2):
                    last_ = cp(ytk[:, 512 * i:512 * i + 512], banks[6 + i][:, :])
                last_.then_inc(S("ytk_ready"), 1)
            xg_out(0)
            pair(0, False)
            with act.Fori(1, NPAIR) as k:
                pair(k, True)
            finish(NPAIR - 1)
            act.wait_ge(S("flag_ready"), 1)
            over_ = act.value_load(flagi[0:1, 0:1], min_val=0, max_val=1)
            with act.If(over_ > 0):
                with act.Fori(NPAIR, NPAIR * NBLK) as k:
                    pair(k, False)
                    finish(k)
            act.nop()
            act.wait_ge(S("yres_done"), 3)
            norms(2, h)

        @block.vector
        def _(dve):
            v = nc.vector
            n = [0]

            def link(ins):
                n[0] += 1
                ins.then_inc(S("dve_chain"), 1)
                dve.wait_ge(S("dve_chain"), n[0])

            def signal(ins, name):
                ins.then_inc(S(name), 1)

            def wait_filled(stage, i):
                dve.wait_ge(S("unit_filled"), U(stage, i + 1))
                return bank(stage, i)

            def norm(k, src, dst, name):
                dve.wait_ge(S("rms"), k + 1)
                link(v.reciprocal(st[:, 3 * k:3 * k + 3], st[:, 3 * k:3 * k + 3]))
                for tile_ in range(3):
                    r_ = TN[tile_]
                    last_ = v.scalar_tensor_tensor(out=dst[0:r_, tile_, :], in0=src[0:r_, tile_, :],
                                                   scalar=st[0:r_, 3 * k + tile_:3 * k + tile_ + 1], in1=gain[0:r_, :],
                                                   op0=ALU.mult, op1=ALU.mult)
                    if name == "y_done":
                        signal(last_, name)
                if name != "y_done":
                    signal(last_, name)
            b = wait_filled("params", 0)
            v.tensor_copy(par[:, :], b[:, 0:NPAR]).then_inc(S("params_ready"), 1)
            dve.wait_ge(S("params_ready"), 1)
            link(v.tensor_tensor(der[:, 0:4], par[:, 0:4], par[:, 4:8], ALU.subtract))
            v.tensor_scalar(der[:, 8:12], par[:, PR["ka"][0]:PR["ka"][0] + 4], -1.0, 1.0, ALU.mult, ALU.add)\
                .then_inc(S("par_ready"), 1)
            dve.wait_ge(S("gain_in"), 16)
            norm(0, h, h, "h_done")
            dve.wait_ge(S("shift_out"), 16 * (NS + 1))
            dve.wait_ge(S("consts_ready"), 1)
            for c in range(KT):
                b = wait_filled("hT", c)
                signal(v.tensor_copy(hT[:, c, :], b[:, 0:NTP]), "hT_ready")
            nraw, nmix = 0, 0
            for n_, (j, _, _) in enumerate(PROJ):
                dve.wait_ge(S("proj_ready"), n_ + 1)
                if j < 4 or 12 <= j < 16:
                    dst = hq[:, j, :] if j < 4 else hg[:, j - 12, :]
                    if j < 4:
                        signal(v.tensor_tensor(dst, dst, raw[:, nraw % 2, 0:NT], ALU.mult), "raw_used")
                    else:
                        v.scalar_tensor_tensor(out=dst, in0=dst, scalar=pcol("gnw"), in1=raw[:, nraw % 2, 0:NT],
                                               op0=ALU.mult, op1=ALU.mult).then_inc(S("raw_used"), 1)
                    nraw += 1
                elif j < 8:
                    dve.wait_ge(S("lb_ready"), 1)
                    if j == 4:
                        link(v.tensor_scalar(der[:, 4:8], der[:, 0:4], -1.0, 1.0, ALU.mult, ALU.add))
                    i = j - 4
                    link(v.tensor_scalar(hf[:, i, :], hf[:, i, :], der[:, 4 + i:5 + i], der[:, i:i + 1], ALU.mult, ALU.add))
                    signal(v.tensor_scalar(hk[:, i, :], hf[:, i, :], -1.0, 1.0, ALU.mult, ALU.add), "hk_ready")
                elif j >= 16:
                    r_ = raw[:, nraw % 2, :]
                    dve.wait_ge(S("dve_chain"), n[0])
                    v.tensor_tensor(dif[:, 1:NT], r_[:, 0:NT - 1], r_[:, 1:NT], ALU.subtract)
                    link(v.tensor_scalar(dif[:, 0:1], r_[:, 0:1], -1.0, None, ALU.mult))
                    link(v.tensor_tensor(dif[:, NP_:NT:TS], r_[:, NT:NTP], r_[:, NP_:NT:TS], ALU.subtract))
                    dst = {4: rr, 5: rk, 6: rv}[j // 4][:, j % 4, :] if j < 28 else lor[:, j - 28, :]
                    ins = v.scalar_tensor_tensor(out=dst, in0=dif[:, :], scalar=pcol("mu", j - 16), in1=r_[:, 0:NT],
                                                 op0=ALU.mult, op1=ALU.add)
                    ins.then_inc(S("raw_used"), 1)
                    nraw += 1
                    dve.wait_ge(S("raw_used"), nraw)
                    if j >= 28:
                        link(v.memset(st[0:1, 15:16], 0.0))
                        v.memset(st[0:1, 15:16], 0.0).then_inc(S("lor_ready"), 1)
                    nmix += 1
                    if nmix == 14:
                        v.memset(st[0:1, 14:15], 0.0).then_inc(S("mixed"), 14)
                if n_ == 13:
                    dve.wait_ge(S("wpre_ready"), 4)
                    dve.wait_ge(S("consts_ready"), 1)
                    for i in range(4):
                        ins = v.tensor_tensor_scan(tA[:, i, :], reset[:, :], rs[:, i, :], 0.0, ALU.mult, ALU.add)
                    link(ins)
                    link(v.tensor_tensor(rs[:, :, :], tA[:, :, :], rs[:, :, :], ALU.subtract))
                    for i in range(2):
                        ins = v.tensor_copy(cen[:, i, :], tA[:, :, P * i + 63])
                    link(ins)
                    for i in range(2):
                        w = slice(P * i, P * i + P)
                        v.tensor_tensor(tA[:, :, w], tA[:, :, w], bc(cen[:, i, :], P), ALU.subtract)
                        ins = v.tensor_tensor(rs[:, :, w], rs[:, :, w], bc(cen[:, i, :], P), ALU.subtract)
                    link(ins)
                    v.memset(st[0:1, 14:15], 0.0).then_inc(S("cen_ready"), 1)
                    v.memset(st[0:1, 13:14], 0.0).then_inc(S("gs_ready"), 1)
                if n_ == 21:
                    dve.wait_ge(S("kss_ready"), 1)
                    for r_, a_, z_ in ((P, 0, 16), (64, 16, 24)):
                        link(v.tensor_scalar(nrm[0:r_, 0, a_:z_], nrm[0:r_, 0, a_:z_], 1e-12, None, ALU.max))
                        ins = v.reciprocal(nrm[0:r_, 1, a_:z_], nrm[0:r_, 0, a_:z_])
                    signal(ins, "kinv_ready")
                if n_ == 25:
                    dve.wait_ge(S("apre_ready"), 4)
                    for i in range(4):
                        b = wait_filled("knb", i)
                        ins = v.scalar_tensor_tensor(out=rkk[:, i, :], in0=rk[:, i, :], scalar=pcol("kk", i), in1=b[:, 0:NT],
                                                     op0=ALU.mult, op1=ALU.mult)
                        signal(ins, "knb_ready")
                        link(v.tensor_scalar(rbon[:, i, :], ra[:, i, :], pcol("ka", i), der[:, 8 + i:9 + i], ALU.mult, ALU.add))
                        link(v.tensor_tensor(rk[:, i, :], rk[:, i, :], rbon[:, i, :], ALU.mult))
                        ins = v.scalar_tensor_tensor(out=rbon[:, i, :], in0=rr[:, i, :], scalar=pcol("rk", i), in1=rk[:, i, :],
                                                     op0=ALU.mult, op1=ALU.mult)
                        signal(ins, "rbon_in")
                    dve.wait_ge(S("knb_ready"), 4)
                    link(v.tensor_tensor(ra[:, :, :], ra[:, :, :], rkk[:, :, :], ALU.mult))
                    dve.wait_ge(S("e3_ready"), 1)
                    v.tensor_tensor(ra[:, :, :], ra[:, :, :], tB[:, :, :], ALU.mult)
                    v.tensor_tensor(rk[:, :, :], rk[:, :, :], tB[:, :, :], ALU.mult)
                    v.scalar_tensor_tensor(out=rkk[:, :, :], in0=rkk[:, :, :], scalar=-1.0, in1=rs[:, :, :],
                                           op0=ALU.mult, op1=ALU.mult)
                    dve.wait_ge(S("e1_ready"), 1)
                    dve.wait_ge(S("rbon_in"), 4)
                    v.tensor_tensor(rr[:, :, :], rr[:, :, :], tA[:, :, :], ALU.mult)
                    for i in range(2):
                        v.tensor_copy(pc[:, :, i], tA[:, :, P * i + P - 1])
                    ins = v.tensor_copy(pc[:, :, 2:10], tA[:, :, NP_ + TS - 1:NT:TS])
                    link(ins)
                    v.tensor_tensor(ec[:, 4:8], pc[:, :, 0], ec[:, 0:4], ALU.mult).then_inc(S("rw_ready"), 1)
            dve.wait_ge(S("raw_used"), nraw)
            dve.wait_ge(S("hk_ready"), 4)
            link(v.memset(at_[:, :], 0.0))
            signal(v.memset(st[0:1, 14:15], 0.0), "at_zero")
            at, seen = 0, 0
            order = LEVELS + [0]
            for i, hh in enumerate(order):
                if i:
                    dve.wait_ge(S("unit_filled"), U("lvl", at))
                if hh:
                    if i:
                        dve.wait_ge(S("pre_ready"), i)
                    v.tensor_tensor(qp[:, :, :], hq[:, :, :], hf[:, :, :], ALU.mult).then_inc(S("qp_ready"), 1)
                    dve.wait_ge(S("suf_ready"), i + 1)
                    dve.wait_ge(S("qp_ready"), i + 1)
                    m = npair(hh)
                    for j in range(4):
                        fv = hf[:, j, 0:m].rearrange("p (b a c) -> p b a c", a=2, c=hh)
                        ins = v.tensor_tensor(fv[:, :, 1, :], fv[:, :, 1, :],
                                              fv[:, :, 0, hh - 1:hh].broadcast_to([P, m // (2 * hh), hh]), ALU.mult)
                    ins.then_inc(S("pre_ready"), 1)
                for tile in range(3 if hh <= 4 else 2):
                    tn = TN[tile]
                    b = wait_filled("lvl", at)
                    msk_ = mT[0:tn, i, 0:tn] if hh else ident[0:tn, 0:tn]
                    if i:
                        dve.wait_ge(S("lvl_ready"), seen)
                    o = at_[0:tn, 512 * tile:512 * tile + 4 * tn].rearrange("p (j t) -> p j t", t=tn)
                    signal(v.copy_predicated(o, rep(msk_.bitcast(I32), 4), b[0:tn, 0:4 * tn].rearrange("p (j t) -> p j t", t=tn)),
                           "lvl_ready")
                    at += 1
                seen = at
            dve.wait_ge(S("lvl_ready"), at)
            dve.wait_ge(S("pre_ready"), 7)
            v.memset(st[0:1, 14:15], 0.0).then_inc(S("at_ready"), 1)
            v.tensor_tensor(qp[:, :, :], hq[:, :, :], hf[:, :, :], ALU.mult).then_inc(S("qp_ready"), 1)
            b = wait_filled("hs2", 0)
            dve.wait_ge(S("unit_filled"), U("ho", 2))
            dve.wait_ge(S("hs1_ready"), 1)
            link(v.tensor_tensor(hs[:, :, :], hs[:, :, :], bc(hf[:, :, NP_ - 1], P), ALU.mult))
            signal(v.tensor_tensor(hs[:, :, :], hs[:, :, :], b[:, :].rearrange("p (h v) -> p h v", v=P), ALU.add), "hs2_ready")
            dve.wait_ge(S("unit_filled"), U("ho", 3))
            for j in range(HGH):
                for half in range(2):
                    o = hs0[:, 4 * half:4 * half + 4, j, :]
                    t0 = NP_ + TS * 4 * half + TS - 1
                    link(v.tensor_tensor(o, o, bc(hf[:, j, t0:t0 + 3 * TS + 1:TS], P), ALU.mult))
                    b = wait_filled("hsend", 2 * j + half)
                    signal(v.tensor_tensor(o, o, b[:, :].rearrange("p (b v) -> p b v", v=P), ALU.add), "hsend_ready")
            dve.wait_ge(S("hvar_ready"), 1)
            v.reciprocal(nrm[:, 2, 0:8], nrm[:, 2, 0:8])
            signal(v.reciprocal(nrm[0:64, 2, 8:12], nrm[0:64, 2, 8:12]), "oinv_ready")
            for j in range(4):
                b = wait_filled("hvarb", j)
                ins = v.tensor_tensor(hq[:, j, :], hq[:, j, :], b[:, 0:NT], ALU.mult)
                signal(ins, "hvarb_ready")
            dve.wait_ge(S("hvarb_ready"), 4)
            v.tensor_tensor(hq[:, :, :], hq[:, :, :], hg[:, :, :], ALU.mult).then_inc(S("mix_hg"), 1)
            for j in range(4):
                b = wait_filled("bonus", j)
                signal(v.tensor_tensor(rbon[:, j, :], rv[:, j, :], b[:, 0:NT], ALU.mult), "bonus_ready")
            dve.wait_ge(S("hgrn_out"), 32)
            dve.wait_ge(S("mix_hg"), 1)
            for stage, dst, m128, m64 in (("gN", mW_, mT[:, 0, :], mT[0:64, 0, 0:64]), ("gK", mK_, strict, strict8),
                                          ("gRb", mRb_, incl, incl8), ("gRk", mRk_, incl, incl8)):
                for x in range(6):
                    tile, p = x // 2, x % 2
                    tn = TN[tile]
                    b = wait_filled(stage, x)
                    m_ = rep((m64 if tile == 2 else m128)[0:tn, 0:tn], 4)
                    ins = v.tensor_tensor(dst(tile, p), b[0:tn, 0:4 * tn].rearrange("p (j t) -> p j t", t=tn), m_, ALU.mult)
                    if stage == "gN":
                        link(ins)
                        ins = v.tensor_tensor(dst(tile, p), dst(tile, p), rep(ident[0:tn, 0:tn], 4), ALU.add)
                    signal(ins, f"{stage}_ready")
            done = {"mZ": 0, "mW": 0, "mT": 0}
            for i, hh in enumerate(LEVELS):
                if hh == 1:
                    continue
                units = [(tile, p) for tile in range(3 if hh <= 4 else 2) for p in range(2)]
                for stage, dst in (("mZ", mZ_), ("mW", mW_), ("mT", mT_)):
                    if stage == "mT" and hh == 64:
                        continue
                    for tile, p in units:
                        tn = TN[tile]
                        b = wait_filled(stage, done[stage])
                        src = b[0:tn, 0:4 * tn].rearrange("p (j t) -> p j t", t=tn)
                        if stage == "mZ":
                            if done["mT"]:
                                dve.wait_ge(S("unit_filled"), U("mT", done["mT"]))
                            ins = v.tensor_tensor(dst(tile, p), src, rep(mT[0:tn, i, 0:tn], 4), ALU.mult)
                        else:
                            if stage == "mW":
                                dve.wait_ge(S("gN_ready"), 6)
                                if done["mW"]:
                                    dve.wait_ge(S("mW_ready"), done["mW"])
                            else:
                                dve.wait_ge(S("T1_ready"), 6)
                                if done["mT"]:
                                    dve.wait_ge(S("mT_ready"), done["mT"])
                            ins = v.tensor_tensor(dst(tile, p), dst(tile, p), src, ALU.add)
                        signal(ins, f"{stage}_ready")
                        done[stage] += 1
            for tile in range(2):
                for p in range(2):
                    rows = slice(64 * p, 64 * p + 64)
                    b = wait_filled("S", 2 * tile + p)
                    o = sp[rows, :].rearrange("p (j v) -> p j v", v=RN)
                    src = b[rows, 0:256].rearrange("p (j v) -> p j v", v=RN)
                    if tile == 0:
                        ins = v.tensor_tensor(o, src, bc(ec[rows, 4:8], RN), ALU.mult)
                    else:
                        dve.wait_ge(S("unit_filled"), U("Y", 4))
                        dve.wait_ge(S("S_ready"), 2)
                        link(v.tensor_tensor(o, o, src, ALU.add))
                        ins = v.tensor_tensor(o, o, bc(pc[rows, :, 1], RN), ALU.mult)
                    signal(ins, "S_ready")
            dve.wait_ge(S("U_ready"), 6)
            for x in range(RWH):
                if x >= 2:
                    dve.wait_ge(*half_done(x - 2))
                v.tensor_tensor(um[0:64, x % 2], rep(uu[0:64, 2, RN * x:RN * x + RN], NS), bc(seqm[:, :], RN), ALU.mult)\
                    .then_inc(S("um_ready"), 1)
            dve.wait_ge(S("unit_filled"), U("Y", 6))
            dve.wait_ge(S("s0t_ready"), 4)
            for j in range(4):
                b = wait_filled("send", j)
                for q in range(4):
                    o = s0t[:, q, j]
                    ins = v.tensor_tensor(o, o, b[:, P * q:P * q + P].rearrange("p (c v) -> p c v", v=RN), ALU.add)
                link(ins)
                for q in range(4):
                    o = s0t[:, q, j]
                    ins = v.tensor_tensor(o, o, bc(pc[:, j, 2 + 2 * q:4 + 2 * q], RN), ALU.mult)
                signal(ins, "send_ready")
            dve.wait_ge(S("Y_ready"), 6)
            for j in range(4):
                b = wait_filled("mean", j)
                ins = v.tensor_tensor(yy[:, j, :], yy[:, j, :], b[:, 0:NT], ALU.subtract)
                signal(ins, "mean_ready")
            dve.wait_ge(S("mean_ready"), 4)
            v.memset(st[0:1, 14:15], 0.0).then_inc(S("yc_ready"), 4)
            dve.wait_ge(S("var_ready"), 1)
            v.reciprocal(nrm[:, 3, 0:16], nrm[:, 2, 0:16])
            signal(v.reciprocal(nrm[0:64, 3, 16:24], nrm[0:64, 2, 16:24]), "yinv_ready")
            dve.wait_ge(S("bonus_ready"), 4)
            dve.wait_ge(S("gpre_ready"), 4)
            for j in range(4):
                b = wait_filled("varb", j)
                ins = v.tensor_tensor(yy[:, j, :], yy[:, j, :], b[:, 0:NT], ALU.mult)
                signal(ins, "varb_ready")
                dve.wait_ge(S("varb_ready"), j + 1)
                link(v.tensor_scalar(yy[:, j, :], yy[:, j, :], pcol("lnw", j), pcol("lnb", j), ALU.mult, ALU.add))
            link(v.tensor_tensor(yy[:, :, :], yy[:, :, :], rbon[:, :, :], ALU.add))
            v.tensor_tensor(yy[:, :, :], yy[:, :, :], rg[:, :, :], ALU.mult).then_inc(S("mixer_done"), 1)
            dve.wait_ge(S("xres_in"), 48)
            for x in range(6):
                tn, tile, half = TN[x // 2], x // 2, x % 2
                b = wait_filled("xo", x)
                o = h[0:tn, tile, 512 * half:512 * half + 512]
                signal(v.tensor_tensor(o, o, b[0:tn, :], ALU.add), "xo_ready")
            dve.wait_ge(S("xo_ready"), 6)
            v.memset(st[0:1, 14:15], 0.0).then_inc(S("xres_done"), 6)
            dve.wait_ge(S("gain2_in"), 16)
            norm(1, h, h2, "h_done")
            v.memset(acc[:, :, :], 0.0).then_inc(S("acc_zero"), 1)
            for c in range(KT):
                b = wait_filled("h2T", c)
                signal(v.tensor_copy(hT[:, c, 0:NT], b[:, 0:NT]), "h2T_ready")
            b = wait_filled("logit", 0)
            dve.wait_ge(S("router_in"), 32)
            for tile in range(3):
                tn = TN[tile]
                ins = v.tensor_tensor(lgt[0:tn, tile, :], b[0:tn, NE * tile:NE * tile + NE], brow[0:tn, :], ALU.add)
            signal(ins, "logit_ready")
            dve.wait_ge(S("logit_ready"), 1)
            for tile in range(3):
                tn = TN[tile]
                link(v.max(top[0:tn, tile, :], lgt[0:tn, tile, :]))
                link(v.max_index(topi[0:tn, tile, :], top[0:tn, tile, :], lgt[0:tn, tile, :]))
                v.tensor_copy(topf[0:tn, tile, :], topi[0:tn, tile, :])
                ins = v.tensor_scalar(gat[0:tn, tile, 0:4], top[0:tn, tile, 0:4], top[0:tn, tile, 0:1], None, ALU.subtract)
                signal(ins, "top_ready")
            dve.wait_ge(S("top_exp"), 3)
            for tile in range(3):
                tn = TN[tile]
                link(v.tensor_reduce(gat[0:tn, tile, 4:5], gat[0:tn, tile, 0:4], AX.X, ALU.add))
                link(v.reciprocal(gat[0:tn, tile, 5:6], gat[0:tn, tile, 4:5]))
                link(v.tensor_scalar(gat[0:tn, tile, 0:4], gat[0:tn, tile, 0:4], gat[0:tn, tile, 5:6], None, ALU.mult))
                for q in range(TOPK):
                    ids, gcol = topf[0:tn, tile, q:q + 1], gat[0:tn, tile, q:q + 1]
                    if q == 0:
                        v.tensor_scalar(msk[0:tn, tile, :], iota[0:tn, 0:NE], ids, None, ALU.is_equal)
                        link(v.tensor_scalar(gate[0:tn, tile, 0:NE], iota[0:tn, 0:NE], ids, gcol, ALU.is_equal, ALU.mult))
                    else:
                        link(v.tensor_scalar(hot[0:tn, :], iota[0:tn, 0:NE], ids, None, ALU.is_equal))
                        v.tensor_tensor(msk[0:tn, tile, :], msk[0:tn, tile, :], hot[0:tn, :], ALU.add)
                        link(v.scalar_tensor_tensor(out=gate[0:tn, tile, 0:NE], in0=hot[0:tn, :], scalar=gcol,
                                                    in1=gate[0:tn, tile, 0:NE], op0=ALU.mult, op1=ALU.add))
                v.memset(st[0:1, 14:15], 0.0).then_inc(S("msk_ready"), 1)
            b = wait_filled("rank", 0)
            for tile in range(3):
                tn = TN[tile]
                link(v.scalar_tensor_tensor(out=rnk[0:tn, tile, 0:NE], in0=msk[0:tn, tile, :], scalar=-FAR,
                                            in1=b[0:tn, NE * tile:NE * tile + NE], op0=ALU.mult, op1=ALU.add))
                link(v.tensor_scalar(rnk[0:tn, tile, 0:NE], rnk[0:tn, tile, 0:NE], FAR, None, ALU.add))
            v.tensor_reduce(flag[0:1, 0:1], b[0:1, 96:96 + NE], AX.X, ALU.max).then_inc(S("rank_ready"), 1)
            dve.wait_ge(S("rank_ready"), 1)
            link(v.tensor_scalar(flag[0:1, 1:2], flag[0:1, 0:1], CAP + 0.5, None, ALU.is_gt))
            v.tensor_copy(flagi[0:1, 0:1], flag[0:1, 1:2]).then_inc(S("flag_ready"), 1)

            def select(k):
                for tile_ in range(3):
                    tn_ = TN[tile_]
                    for s in range(2):
                        last_ = v.tensor_scalar(sel[0:tn_, tile_, CAP * s:CAP * s + CAP],
                                                iota[0:tn_, bass.ds((k >> 4) * CAP, CAP)],
                                                rnk[0:tn_, tile_, bass.ds((k & (NPAIR - 1)) * 2 + s, 1)], None, ALU.is_equal)
                signal(last_, "sel_ready")

            def select_gates(k):
                dve.wait_ge(S("selg_turned"), k)
                for tile_ in range(3):
                    tn_ = TN[tile_]
                    for s in range(2):
                        ei = (k & (NPAIR - 1)) * 2 + s
                        last_ = v.tensor_scalar(selg[0:tn_, tile_, CAP * s:CAP * s + CAP],
                                                iota[0:tn_, bass.ds((k >> 4) * CAP, CAP)],
                                                rnk[0:tn_, tile_, bass.ds(ei, 1)], gate[0:tn_, tile_, bass.ds(ei, 1)],
                                                ALU.is_equal, ALU.mult)
                signal(last_, "selg_ready")

            def swiglu(k, ab):
                e = k * 2 + ab
                ex = e & (NE - 1)
                dve.wait_ge(S("used3"), e + 1)
                for i in range(2):
                    cs, n = slice(4 * i, 4 * i + 4), 2 * e + i
                    bs = slice(4 * i * CAP, 4 * (i + 1) * CAP)
                    dve.wait_ge(S("h1_ready"), n)
                    v.tensor_tensor(gg[:, cs, :], banks[0][:, bs].rearrange("p (c s) -> p c s", s=CAP),
                                    bc(bgu[:, bass.ds(ex * 16 + 4 * i, 4)], CAP), ALU.add).then_inc(S("g1"), 1)
                    v.tensor_tensor(upv[:, cs, :], banks[1][:, bs].rearrange("p (c s) -> p c s", s=CAP),
                                    bc(bgu[:, bass.ds(ex * 16 + 8 + 4 * i, 4)], CAP), ALU.add).then_inc(S("gu_read"), 1)
                    dve.wait_ge(S("g1"), n + 1)
                    v.tensor_scalar(gg[:, cs, :], gg[:, cs, :], LIMIT, None, ALU.min).then_inc(S("gate_ready"), 1)
                    dve.wait_ge(S("gu_read"), n + 1)
                    v.tensor_scalar(upv[:, cs, :], upv[:, cs, :], LIMIT, -LIMIT, ALU.min, ALU.max).then_inc(S("up_clip"), 1)
                    dve.wait_ge(S("sig_ready"), n + 1)
                    dve.wait_ge(S("gate_ready"), n + 1)
                    v.tensor_tensor(gg[:, cs, :], gg[:, cs, :], sg[:, cs, :], ALU.mult).then_inc(S("glu_done"), 1)
                    dve.wait_ge(S("glu_done"), n + 1)
                    dve.wait_ge(S("up_clip"), n + 1)
                    v.scalar_tensor_tensor(out=h1[:, ab, cs, :], in0=upv[:, cs, :], scalar=1.0, in1=gg[:, cs, :],
                                           op0=ALU.add, op1=ALU.mult).then_inc(S("h1_ready"), 1)

            def output(k, ab):
                e = k * 2 + ab
                dve.wait_ge(S("used5"), e + 1)
                if ab == 0:
                    dve.wait_ge(S("y_turned"), k)
                v.tensor_tensor(yt[:, :, CAP * ab:CAP * ab + CAP], banks[5][:, :].rearrange("p (c s) -> p c s", s=CAP),
                                bc(bdn[:, bass.ds((e & (NE - 1)) * 8, 8)], CAP), ALU.add).then_inc(S("y_read"), 1)

            def finish(k):
                for c in range(KT):
                    dve.wait_ge(S("scattered"), 8 * k + c + 1)
                    v.tensor_tensor(acc[:, c, :], acc[:, c, :], banks[6 + c % 2][:, 0:NT], ALU.add).then_inc(S("acc_added"), 1)

            def pair(k, before):
                if before:
                    finish(k - 1)
                swiglu(k, 0)
                select_gates(k)
                output(k, 0)
                swiglu(k, 1)
                dve.wait_ge(S("gathered"), 2 * k + 4)
                select(k + 2)
                output(k, 1)
            dve.wait_ge(S("acc_zero"), 1)
            select(0)
            dve.wait_ge(S("gathered"), 2)
            select(1)
            pair(0, False)
            with dve.Fori(1, NPAIR) as k:
                pair(k, True)
            finish(NPAIR - 1)
            over_ = dve.value_load(flagi[0:1, 0:1], min_val=0, max_val=1)
            with dve.If(over_ > 0):
                with dve.Fori(NPAIR, NPAIR * NBLK) as k:
                    pair(k, False)
                    finish(k)
            dve.nop()
            v.memset(st[0:1, 14:15], 0.0).then_inc(S("acc_done"), 1)
            for tile in range(3):
                tn = TN[tile]
                dve.wait_ge(S("acc_turned"), tile + 1)
                for i in range(2):
                    o = h[0:tn, tile, 512 * i:512 * i + 512]
                    ins = v.tensor_tensor(o, o, banks[2 * tile + i][0:tn, :], ALU.add)
                ins.then_inc(S("yres_done"), 1)
            dve.wait_ge(S("gain3_in"), 16)
            norm(2, h, yrow, "y_done")


_INS = ["x_prompt", "x_sample", "state_hgrn", "state_rwkv", "state_shift", "norm_mix", "w_in", "lb_logits", "hg_norm_w",
        "rw_mu", "rw_w0", "rw_w2", "rw_a0", "rw_a2", "rw_g2", "rw_k_k", "rw_k_a", "rw_r_k", "rw_lnx_w", "rw_lnx_b",
        "w_out", "norm_ffn", "w_router", "b_router", "w_gate_up", "b_gate_up", "w_down", "b_down", "norm_final"]
_OUTS = [(1, NP_, DM), (NS, TS, DM), (1, 1, HGH, P, P), (1, 1, RWH, RN, RN), (1, 1, DM),
         (1, NS, HGH, P, P), (1, NS, RWH, RN, RN), (1, NS, DM)]


def kernel(**inputs):
    import numpy as _np
    import concourse.bacc as _bacc
    from concourse import mybir as _mybir
    from concourse.bass_utils import run_bass_kernel_spmd as _run

    nc = _bacc.Bacc("TRN2", target_bir_lowering=False, num_devices=1)
    arrays, ins = {}, {}
    for name in _INS:
        a = _np.ascontiguousarray(inputs[name])
        arrays[f"in_{name}"] = a
        ins[name] = nc.dram_tensor(f"in_{name}", a.shape, _mybir.dt.from_np(a.dtype), kind="ExternalInput").ap()
    outs = [nc.dram_tensor(f"out_{i}", s, _mybir.dt.float32, kind="ExternalOutput").ap() for i, s in enumerate(_OUTS)]
    build(nc, ins, outs)
    r = _run(nc, [arrays], core_ids=[0])
    return tuple(r.results[0][f"out_{i}"] for i in range(len(_OUTS)))
```

```python
import math
from contextlib import ExitStack

import concourse.bass as bass
from concourse import mybir

P = 128
F32 = mybir.dt.float32
F32R = mybir.dt.float32r
I32 = mybir.dt.int32
U32 = mybir.dt.uint32
ALU = mybir.AluOpType
ACT = mybir.ActivationFunctionType
AX = mybir.AxisListType

DM = 1024
KT = DM // P
NP_, NS, TS = 256, 8, 8
NT = NP_ + NS * TS
NTP = NT + NS
TOFF, TN = [0, 128, 256], [128, 128, 64]
HGH, RWH, RN = 4, 8, 64
WIN = 3840
WORDER = [5, 7, 4, 6, 1, 0, 2, 3]
NE, TOPK, DFF = 32, 4, 1024
CAP = 64
NBLK = NT // CAP
CHUNK = 4096
NCOL = 512
PIECE = KT // 2 * NCOL
NW, NHI, NLO = 6, 4, 3
EARLY = [2, 2, 3, 2]
BIAS_BANKS = [0, 1, 2, 3, 6, 7]
NWR = 3
GROUPS = [0, 2, 1, 3]
NG = len(GROUPS) + DM // NCOL
NPC = 2 * NG
EPS, GN_EPS = 1e-6, 64e-5
EDEC = math.exp(-0.5)
LIMIT, ALPHA = 7.0, 1.702
LEVELS = [1, 2, 4, 8, 16, 32, 64]
FAR = 4096.0

PR = {}
_n = 0
for _name, _k in (("lb0", 4), ("lb1", 4), ("mu", 14), ("w0", 4), ("a0", 4), ("kk", 4), ("ka", 4), ("rk", 4),
                  ("lnw", 4), ("lnb", 4), ("gnw", 1)):
    PR[_name] = (_n, _k)
    _n += _k
NPAR = _n


def proj_tiles():
    out = []
    for n, g in enumerate(WORDER):
        for i in range(2 if g == 7 else 4):
            out.append((4 * g + i, n, i))
    return out


PROJ = proj_tiles()
LATE = 2
PPOS = {j: n for n, (j, _, _) in enumerate(PROJ)}


def psum_units():
    u = []

    def add(stage, n):
        k = sum(1 for s, _ in u if s == stage)
        u.extend((stage, k + i) for i in range(n))
    add("params", 1)
    add("hT", KT)
    add("proj", 14)
    add("wpre", 4)
    add("apre", 4)
    add("gpre", 4)
    add("proj", 8)
    add("kss", 1)
    add("proj", 4)
    add("knb", 4)
    add("proj", len(PROJ) - LATE - 26)
    add("itok", 3)
    for i, h in enumerate(LEVELS):
        add("lvl", 3 if h <= 4 else 2)
        if i < LATE:
            add("proj", 1)
    add("lvl", 3)
    add("kstok", 3)
    add("hs1", 1)
    add("ho", 3)
    add("hs2", 1)
    add("hsend", 8)
    add("hvar", 1)
    add("hvarb", 4)
    add("bonus", 4)
    add("s0t", 4)
    add("vtok", 3)
    add("btok", 3)
    add("ktok", 3)
    for s in ("gM", "gN", "gK", "gRb", "gRk"):
        add(s, 6)
    for h in LEVELS[1:]:
        n = 6 if h <= 4 else 4
        add("mZ", n)
        add("mW", n)
        if h < 64:
            add("mT", n)
    add("rst", 2)
    for tile in range(3):
        add("R", 2)
        add("U", 2)
        add("Y", 2)
        if tile < 2:
            add("S", 2)
    add("send", 4)
    add("pst", 1)
    add("sout", 4)
    add("mean", 4)
    add("var", 1)
    add("varb", 4)
    add("xo", 6)
    add("bias", 1)
    add("h2T", KT)
    add("logit", 1)
    add("rank", 1)
    add("gT", 1)
    return u


UNITS = psum_units()
UPOS = {k: n for n, k in enumerate(UNITS)}


def unit_banks():
    at, before, had = [], [], {}
    few = UPOS["send", 0], UPOS["xo", 0]
    for n in range(len(UNITS)):
        if few[0] <= n < few[1]:
            b = (n - few[0]) % 4
        elif n >= few[1]:
            b = (n - few[1] + 4) % 8
        else:
            b = n % 8
        at.append(b)
        before.append(had.get(b))
        had[b] = n
    return at, before


BANK, BEFORE = unit_banks()


def build(nc, A, O):
    ctx = ExitStack()
    with ctx:
        def sb(name, shape, dt=F32):
            return ctx.enter_context(nc.sbuf_tensor(name, shape, dt))

        sems = {}

        def S(name):
            if name not in sems:
                sems[name] = ctx.enter_context(nc.semaphore(name))
            return sems[name]

        with nc.sbuf_tensor("ring", [P, 6 * CHUNK], F32, side="right") as ring:
            pass

        def later(name, n, dt):
            return ctx.enter_context(nc.sbuf_tensor(name, [P, n], dt, side="right"))
        gupb = later("gate_up_sums", 2 * NCOL, F32)
        h1b = later("hidden_parts", KT * P, F32R)
        xgb = later("token_parts", 2 * KT * P, F32R)
        lob = later("low_parts", NLO * PIECE, F32R)
        wrb = later("raw_pieces", NWR * PIECE, F32)
        hib = later("high_parts", NHI * PIECE, F32R)

        def slot(i):
            return ring[:, i * CHUNK:(i + 1) * CHUNK]
        OV = 2 * CHUNK

        def over(at, n):
            return ring[:, OV + at:OV + at + n]
        W5 = HGH * NT
        mix = sb("mix", [P, 13 * W5])

        def marr(i):
            return mix[:, i * W5:(i + 1) * W5].rearrange("p (j t) -> p j t", t=NT)
        hq, hf, hk, hi, hg = (marr(i) for i in range(5))
        rr, rk, rv, rg, rs, ra, rkk, rbon = (marr(i) for i in range(5, 13))
        hx = sb("hx", [P, 3 * DM])
        h = hx[:, :].rearrange("p (a d) -> p a d", d=DM)
        tA = hx[:, 0:W5].rearrange("p (j t) -> p j t", t=NT)
        tB = hx[:, W5:2 * W5].rearrange("p (j t) -> p j t", t=NT)
        hTb = sb("hTb", [P, KT * NTP])
        hT = hTb[:, :].rearrange("p (c t) -> p c t", t=NTP)
        ident = sb("ident", [P, P])
        ones = sb("ones", [P, P])
        blk = sb("blk", [P, P])
        blkm = sb("blkm", [P, P])
        mT = sb("mT", [P, len(LEVELS), P])
        mM = sb("mM", [P, P])
        strict = sb("strict", [P, P])
        incl = sb("incl", [P, P])
        strict8 = sb("strict8", [64, 64])
        incl8 = sb("incl8", [64, 64])
        seqm = sb("seqm", [64, NS])
        reset = rbon[:, 0, :]
        iota = sb("iota", [P, (NBLK + 2) * CAP])
        epst = sb("epst", [P, 2])
        gain = hTb[:, 0:DM]
        prow = hTb[:, 2 * DM:2 * DM + P]
        par = sb("par", [P, NPAR])
        der = sb("der", [P, 12])
        raw = sb("raw", [P, 2, NTP])
        dif = hx[:, 2 * W5:2 * W5 + NT]
        lor = sb("lor", [P, 2, NT])
        iotai = lor[:, :, :].rearrange("p a t -> p (a t)")[:, 0:(NBLK + 2) * CAP].bitcast(I32)
        junk = hTb[:, DM:2 * DM]
        w2a2 = sb("w2a2", [P, NE * 16])
        bgu = w2a2
        g2w = sb("g2w", [P, 512])
        st = sb("st", [P, 16])
        nrm = sb("nrm", [P, 4, 24])
        cen = sb("cen", [P, 2, 4])
        pc = sb("pc", [P, 4, 10])
        ec = sb("ec", [P, 8])
        sp = sb("sp", [P, 256])
        pout = g2w[0:64, :]

        def pcol(name, i=0):
            a, _ = PR[name]
            return par[:, a + i:a + i + 1]
        banks = [ctx.enter_context(nc.psum_tensor(f"bank{i}", [P, 512], F32)) for i in range(8)]

        def U(stage, k):
            return UPOS[stage, k - 1] + 1

        def half_done(x):
            return (S("send_half"), x // 2 + 1) if x % 2 == 0 else (S("unit_filled"), U("send", x // 2 + 1))

        def bank(stage, i):
            return banks[BANK[UPOS[stage, i]]]

        suf = over(0, W5).rearrange("p (j t) -> p j t", t=NT)
        qp = over(W5, W5).rearrange("p (j t) -> p j t", t=NT)
        ks = over(2 * W5, W5).rearrange("p (j t) -> p j t", t=NT)
        at_ = over(3 * W5, W5)
        itok = over(4 * W5, 1536).rearrange("p (a d) -> p a d", d=512)
        kstok = over(4 * W5 + 1536, 1536).rearrange("p (a d) -> p a d", d=512)
        hs0 = over(4 * W5 + 3072, 4096).rearrange("p (b h v) -> p b h v", b=NS, h=HGH)
        hs = over(4 * W5 + 7168, 512).rearrange("p (h v) -> p h v", v=P)
        imask = over(4 * W5 + 7680, 2048).rearrange("p (n b v) -> p n b v", n=2, v=P)
        MW = 2560

        def mats(t):
            def unit(tile, p, part=None):
                n = TN[tile]
                o = 1024 * tile + p * 4 * n
                return t[0:n, o:o + 4 * n].rearrange("p (j t) -> p j t", t=n)
            return unit
        mM_, mT_, mW_, mZ_, mK_, mRb_ = (mats(over(i * MW, MW)) for i in range(6))
        mRk_ = mats(mix[:, W5:W5 + MW])
        vtok = hTb[:, 0:1536].rearrange("p (a d) -> p a d", d=512)
        s0raw = hTb[:, 0:2048].rearrange("p (b h k) -> p b h k", b=4, h=RWH)
        btok = hx[:, 0:1536].rearrange("p (a d) -> p a d", d=512)
        ktok = hx[:, 1536:3072].rearrange("p (a d) -> p a d", d=512)
        s0t = mix[:, 3 * W5:3 * W5 + 2048].rearrange("p (b j c v) -> p b j c v", b=4, j=4, c=2)
        uu = over(0, 1536).rearrange("p (a d) -> p a d", d=512)
        rR = over(3 * MW, 1536).rearrange("p (a d) -> p a d", d=512)
        um = over(MW, 1024).rearrange("p (n b v) -> p n b v", n=2, v=RN)
        vm = over(MW + 1024, 1024).rearrange("p (n b v) -> p n b v", n=2, v=RN)
        rst = over(3 * MW + 1536, 256).rearrange("p (j t) -> p j t", t=64)
        sout = over(4 * MW, 2048).rearrange("p (b j k) -> p b j k", b=4, j=4)
        yy = rk
        xres = h
        h2 = mix[:, 9 * W5:9 * W5 + 3072].rearrange("p (a d) -> p a d", d=DM)
        acc = mix[:, W5:W5 + KT * NT].rearrange("p (c t) -> p c t", t=NT)
        wr = sb("wr", [P, KT, NE])
        brow = sb("brow", [P, NE])
        lgt = sb("lgt", [P, 3, NE])
        top = sb("top", [P, 3, 8])
        topi = sb("topi", [P, 3, 8], U32)
        topf = sb("topf", [P, 3, 8])
        gat = sb("gat", [P, 3, 8])
        hot = sb("hot", [P, NE])
        msk = sb("msk", [P, 3, NE])
        gate = sb("gate", [P, 3, NE + 2])
        rnk = sb("rnk", [P, 3, NE + 2])
        flag = sb("flag", [P, 2])
        flagi = sb("flagi", [1, 1], I32)
        twin = sb("twin", [P, CAP])
        E0 = 3 * W5
        brows = mix[:, E0:E0 + 512].rearrange("p (a d) -> p a d", d=P)
        bdr = mix[0:NE, E0 + 512:E0 + 1536]
        sel = mix[:, E0 + 1536:E0 + 1920].rearrange("p (a c) -> p a c", c=P)
        selg = mix[:, E0 + 1920:E0 + 2304].rearrange("p (a n s) -> p a n s", n=2, s=CAP)
        scat = mix[:, E0 + 2304:E0 + 2624]
        upv = mix[:, E0 + 2624:E0 + 3136].rearrange("p (c s) -> p c s", s=CAP)
        gateT = mix[0:NE, E0 + 3136:E0 + 3456]
        R0, X0 = E0 + 3456, 9 * W5 + 3 * DM
        assert R0 + 2 * PIECE <= 9 * W5 and X0 + PIECE <= 13 * W5
        gg = mix[:, 0:512].rearrange("p (c s) -> p c s", s=CAP)
        sg = mix[:, 512:1024].rearrange("p (c s) -> p c s", s=CAP)
        ytk = junk

        def pieces(t, at, n):
            return [t[:, at + PIECE * i:at + PIECE * (i + 1)].rearrange("p (c n) -> p c n", n=NCOL) for i in range(n)]
        w32 = pieces(wrb, 0, NWR) + pieces(mix, R0, 2) + pieces(mix, X0, 1)
        whi, wlo = pieces(hib, 0, NHI), pieces(lob, 0, NLO)
        gup = gupb[:, :].rearrange("p (n d) -> p n d", n=2)
        xg = xgb[:, :].rearrange("p (c b n s) -> p c b n s", c=KT, b=2, n=2)
        h1 = h1b[:, :].rearrange("p (c n s) -> p c n s", n=2, s=CAP)
        yrow = ring[:, 0:3 * DM].rearrange("p (a d) -> p a d", d=DM)

        def bc(ap, n):
            return ap.unsqueeze(2).broadcast_to([ap.shape[0], ap.shape[1], n])

        def rep(ap, n):
            return ap.unsqueeze(1).broadcast_to([ap.shape[0], n, ap.shape[1]])

        def npair(h_):
            return NT if h_ <= 4 else NP_

        NPAIR = NE // 2

        block = ctx.enter_context(nc.Block())

        @block.sync
        def _(sync):
            def load(dst, src, name):
                sync.dma_start(dst, src).then_inc(S(name), 16)

            def params(name, src):
                a, k = PR[name]
                load(prow[a:a + k, :], src, "prow_in")
            xp, xs = A["x_prompt"], A["x_sample"]
            load(h[:, 0, :], xp[0, 0:P, :], "x_in")
            load(h[:, 1, :], xp[0, P:2 * P, :], "x_in")
            load(h[0:64, 2, :], xs.rearrange("b t d -> (b t) d"), "x_in")
            load(h[64:72, 2, :], A["state_shift"][0], "x_in")
            load(gain[:, :], A["norm_mix"].broadcast_to([P, DM]), "gain_in")
            params("lb0", A["lb_logits"][0:1, :].rearrange("a (h p) -> (a h) p", p=P))
            params("lb1", A["lb_logits"][1:2, :].rearrange("a (h p) -> (a h) p", p=P))
            for nm, src in (("mu", "rw_mu"), ("w0", "rw_w0"), ("a0", "rw_a0"), ("kk", "rw_k_k"), ("ka", "rw_k_a"),
                            ("lnw", "rw_lnx_w"), ("lnb", "rw_lnx_b")):
                params(nm, A[src].rearrange("a (h p) -> (a h) p", p=P))
            params("rk", A["rw_r_k"][0].rearrange("(j h) n -> j (h n)", h=2))
            params("gnw", A["hg_norm_w"])
            w_in = A["w_in"][0].rearrange("(c p) n -> p c n", p=P)
            for n, g in enumerate(WORDER):
                if n >= 6:
                    last = max(i for i, (_, m, _) in enumerate(PROJ) if m == n - 6)
                    sync.wait_ge(S("unit_filled"), U("proj", last + 1))
                if n == 3:
                    sync.wait_ge(S("h_done"), 3)
                    sync.dma_start(O[4][0], h[P - 1:P, 1, :]).then_inc(S("shift_out"), 16)
                    for b in range(NS):
                        sync.dma_start(O[7][0, b:b + 1, :], h[TS * b + TS - 1:TS * b + TS, 2, :]).then_inc(S("shift_out"), 16)
                w = 256 if g == 7 else 512
                load(slot(n % 6).rearrange("p (c n) -> p c n", c=KT)[:, :, 0:w], w_in[:, :, 512 * g:512 * g + w], f"ring{n % 6}")
                if n == 1:
                    load(w2a2[0:64, :], A["rw_w2"][0], "lora_in")
                    load(w2a2[64:128, :], A["rw_a2"][0], "lora_in")
                    load(g2w[:, :], A["rw_g2"][0], "lora_in")
            sync.wait_ge(S("unit_filled"), U("proj", PPOS[4 * WORDER[5] + 3] + 1))
            load(hs0, A["state_hgrn"][0].rearrange("b h k v -> k b h v"), "hs0_in")
            sync.wait_ge(S("unit_filled"), U("proj", 30))
            w_out = A["w_out"][0].rearrange("(c p) n -> p c n", p=P)
            for i in range(2):
                load(slot(i).rearrange("p (c n) -> p c n", n=DM), w_out[:, 4 * i:4 * i + 4, :], f"ring{i}")
            srw = A["state_rwkv"][0].rearrange("(b c) h v k -> c v b h k", c=2)
            for c in range(2):
                for q in range(4):
                    load(s0raw[64 * c:64 * c + 64, q], srw[c][:, q], "s0_in")
            load(wr[:, :, :], A["w_router"][0].rearrange("(c p) n -> p c n", p=P), "router_in")
            load(brow[:, :], A["b_router"].broadcast_to([P, NE]), "router_in")
            sync.wait_ge(S("unit_filled"), U("send", 4))
            load(h[:, 0, :], xp[0, 0:P, :], "xres_in")
            load(h[:, 1, :], xp[0, P:2 * P, :], "xres_in")
            load(h[0:64, 2, :], xs.rearrange("b t d -> (b t) d"), "xres_in")
            sync.wait_ge(S("send_ready"), 4)
            sync.wait_ge(S("unit_filled"), U("sout", 4))
            bg = A["b_gate_up"][0].rearrange("e (c p) -> (e c) p", p=P)
            load(brows[:, 0:4, :], bg.rearrange("(a q) p -> q a p", q=P), "brow_in")
            load(bdr, A["b_down"][0], "brow_in")
            load(gain[:, :], A["norm_ffn"].broadcast_to([P, DM]), "gain2_in")

            wgu = A["w_gate_up"][0].rearrange("e (c p) n -> p e c n", p=P)
            wdn = A["w_down"][0].rearrange("e (c p) n -> p e c n", p=P)

            def piece(e, i, n):
                j, cs = i // 2, slice(4 * (i % 2), 4 * (i % 2) + 4)
                if j < len(GROUPS):
                    src = wgu[:, e, cs, NCOL * GROUPS[j]:NCOL * (GROUPS[j] + 1)]
                else:
                    j -= len(GROUPS)
                    src = wdn[:, e, cs, NCOL * j:NCOL * (j + 1)]
                load(w32[n], src, f"w{n}_in")

            def expert(e, x):
                for i in range(NPC):
                    n = i % NW
                    if isinstance(e, int) and e == 0 and i < NW:
                        continue
                    sync.wait_ge(S("lo_pool"), NPC * e + i - NW + 2)
                    sync.wait_ge(S(f"w{n}_in"), 16)
                    piece(x, i, n)
            sync.wait_ge(S("mixer_done"), 1)
            sync.wait_ge(S("rwkv_out"), 128)
            for i in range(NW):
                if i == NWR:
                    sync.wait_ge(S("unit_filled"), U("xo", 6))
                piece(0, i, i)
            sync.wait_ge(S("unit_filled"), U("logit", 1))
            load(gain[:, :], A["norm_final"].rearrange("(a d) -> a d", a=1).broadcast_to([P, DM]), "gain3_in")
            expert(0, 0)
            with sync.Fori(1, NE) as e:
                expert(e, e)
            sync.wait_ge(S("flag_ready"), 1)
            over_ = sync.value_load(flagi[0:1, 0:1], min_val=0, max_val=1)
            with sync.If(over_ > 0):
                with sync.Fori(1, NBLK) as n:
                    with sync.Fori(0, NE) as x:
                        expert(n * NE + x, x)
            sync.nop()
            for tile in range(3):
                sync.wait_ge(S("y_done"), tile + 1)
                dst = (O[0][0, P * tile:P * tile + P, :] if tile < 2 else O[1].rearrange("b t d -> (b t) d"))
                sync.dma_start(dst, yrow[0:TN[tile], tile, :]).then_inc(S("y_out"), 16)
            sync.wait_ge(S("y_out"), 48)

        @block.gpsimd
        def _(pool):
            n = [0]

            def link(ins):
                n[0] += 1
                ins.then_inc(S("pool_chain"), 1)
                pool.wait_ge(S("pool_chain"), n[0])
            g = nc.gpsimd
            link(g.memset(ones[:, :], 1.0))
            link(g.memset(ident[:, :], 0.0))
            link(g.memset(blk[:, :], 0.0))
            link(g.memset(blkm[:, :], 0.0))
            link(g.memset(mT[:, :, :], 0.0))
            link(g.memset(mM[:, :], 0.0))
            link(g.memset(reset[:, :], 1.0))
            link(g.memset(epst[:, 0:1], EPS))
            link(g.memset(epst[:, 1:2], GN_EPS))
            link(g.memset(st[:, :], 1.0))
            link(g.memset(blk[0:64, 0:64], 1.0))
            link(g.memset(blk[64:128, 64:128], 1.0))
            link(g.memset(blkm[0:64, 0:64], 1.0 / RN))
            link(g.memset(blkm[64:128, 64:128], 1.0 / RN))
            link(g.memset(reset[:, 0:P + 1:P], 0.0))
            link(g.memset(reset[:, NP_:NT:TS], 0.0))
            link(g.affine_select(out=ident[:, :], in_=ident[:, :], compare_op=ALU.not_equal, fill=1.0, base=0,
                                 pattern=[[-1, P]], channel_multiplier=1))
            g.memset(st[0:1, 15:16], 1.0).then_inc(S("ident_ready"), 1)

            def select(out, in_, pattern, base, ch):
                link(g.affine_select(out=out, in_=in_, compare_op=ALU.is_ge, fill=0.0, base=base, pattern=pattern,
                                     channel_multiplier=ch))
            for i, hh in enumerate(LEVELS):
                nb = P // (2 * hh)
                v = mT[:, i, :].rearrange("p (b a c) -> p b a c", a=2, c=hh)[:, :, 1, :]
                o = ones[:, 0:nb * hh].rearrange("p (b c) -> p b c", c=hh)
                select(v, o, [[-2 * hh, nb], [0, hh]], 0, 1)
                select(v, v, [[2 * hh, nb], [0, hh]], hh - 1, -1)
            v = mM[:, :].rearrange("p (b a) -> p b a", a=2)[:, :, 0:1]
            o = ones[:, 0:64].rearrange("p (b c) -> p b c", c=1)
            select(v, o, [[-2, 64], [0, 1]], -1, 1)
            select(v, v, [[2, 64], [0, 1]], 1, -1)
            select(strict[:, :], ones[:, :], [[1, P]], -1, -1)
            select(incl[:, :], ones[:, :], [[1, P]], 0, -1)
            s8 = strict8[:, :].rearrange("p (b c) -> p b c", c=TS)
            i8 = incl8[:, :].rearrange("p (b c) -> p b c", c=TS)
            o8 = ones[0:64, 0:64].rearrange("p (b c) -> p b c", c=TS)
            select(s8, o8, [[-TS, NS], [0, TS]], 0, 1)
            select(s8, s8, [[TS, NS], [1, TS]], -1, -1)
            select(i8, o8, [[-TS, NS], [0, TS]], 0, 1)
            select(i8, i8, [[TS, NS], [1, TS]], 0, -1)
            select(seqm[:, :], ones[0:64, 0:NS], [[-TS, NS]], 0, 1)
            select(seqm[:, :], seqm[:, :], [[TS, NS]], TS - 1, -1)
            link(g.iota(iotai[:, :], [[1, (NBLK + 2) * CAP]], base=0, channel_multiplier=0))
            g.tensor_copy(iota[:, :], iotai[:, :]).then_inc(S("consts_ready"), 1)

            pool.wait_ge(S("hk_ready"), 4)
            pool.wait_ge(S("unit_filled"), U("proj", PPOS[4 * WORDER[5] + 3] + 1))
            link(g.memset(suf[:, :, :], 1.0))
            pool.wait_ge(S("at_zero"), 1)
            for i, hh in enumerate(LEVELS):
                if i:
                    pool.wait_ge(S("unit_filled"), U("lvl", sum(3 if x <= 4 else 2 for x in LEVELS[:i])))
                    g.tensor_tensor(ks[:, :, :], hk[:, :, :], suf[:, :, :], ALU.mult).then_inc(S("ks_ready"), 1)
                    pool.wait_ge(S("ks_ready"), i)
                m = npair(hh)
                sv = suf[:, :, 0:m].rearrange("p j (b a c) -> p j b a c", a=2, c=hh)
                fv = hf[:, :, 0:m].rearrange("p j (b a c) -> p j b a c", a=2, c=hh)
                for j in range(4):
                    out = sv[:, j, :, 0, :]
                    tot = fv[:, j, :, 1, hh - 1:hh].broadcast_to([P, m // (2 * hh), hh])
                    last = g.tensor_tensor(out, out, tot, ALU.mult)
                    if j < 3:
                        link(last)
                last.then_inc(S("suf_ready"), 1)
                pool.wait_ge(S("suf_ready"), i + 1)
                pool.wait_ge(S("pre_ready"), i + 1)
            pool.wait_ge(S("unit_filled"), U("lvl", sum(3 if x <= 4 else 2 for x in LEVELS) + 3))
            g.tensor_tensor(ks[:, :, :], hk[:, :, :], suf[:, :, :], ALU.mult).then_inc(S("ks_ready"), 1)
            pool.wait_ge(S("ks_ready"), len(LEVELS))
            for j in range(HGH):
                pool.wait_ge(S("itok_ready"), 3)
                if j >= 2:
                    pool.wait_ge(S("unit_filled"), U("hsend", 2 * (j - 1)))
                g.tensor_tensor(imask[0:64, j % 2], rep(itok[0:64, 2, P * j:P * j + P], NS), bc(seqm[:, :], P),
                                ALU.mult).then_inc(S("imask_ready"), 1)
                pool.wait_ge(S("imask_ready"), j + 1)
            pool.wait_ge(S("hs2_ready"), 1)
            pool.dma_start(O[2][0, 0].rearrange("h k v -> k h v"), hs[:, :, :]).then_inc(S("hgrn_out"), 16)
            pool.wait_ge(S("hsend_ready"), 8)
            pool.dma_start(O[5][0].rearrange("b h k v -> k b h v"), hs0).then_inc(S("hgrn_out"), 16)
            pool.wait_ge(S("hgrn_out"), 32)
            for tile in range(3):
                for p in range(2):
                    tn = TN[tile]
                    pool.wait_ge(S("gM_ready"), 2 * tile + p + 1)
                    link(g.tensor_tensor(mT_(tile, p), mM_(tile, p), rep(mM[0:tn, 0:tn], 4), ALU.mult))
                    g.tensor_tensor(mT_(tile, p), mT_(tile, p), rep(ident[0:tn, 0:tn], 4), ALU.add)\
                        .then_inc(S("T1_ready"), 1)
                    pool.wait_ge(S("T1_ready"), 2 * tile + p + 1)
            pool.wait_ge(S("vtok_ready"), 3)
            pool.wait_ge(S("mW_ready"), 2 * 6 + 4 * 4)
            for x in range(RWH):
                if x >= 2:
                    pool.wait_ge(*half_done(x - 2))
                g.tensor_tensor(vm[0:64, x % 2], rep(vtok[0:64, 2, RN * x:RN * x + RN], NS), bc(seqm[:, :], RN),
                                ALU.mult).then_inc(S("vm_ready"), 1)
                pool.wait_ge(S("vm_ready"), x + 1)
            pool.wait_ge(S("pst_ready"), 1)
            pool.dma_start(O[3][0, 0].rearrange("h v k -> v h k"), pout[:, :].rearrange("p (h k) -> p h k", k=RN))\
                .then_inc(S("prompt_state_out"), 16)
            pool.wait_ge(S("sout_ready"), 4)
            ors = O[6][0].rearrange("(b c) h v k -> c v b h k", c=2)
            for c in range(2):
                for q in range(4):
                    pool.dma_start(ors[c][:, q], sout[64 * c:64 * c + 64, q].rearrange("p j (h k) -> p (j h) k", h=2))\
                        .then_inc(S("rwkv_out"), 16)
            def pair(k):
                for i in range(2 * NPC):
                    pool.wait_ge(S("hi_ready"), 2 * NPC * k + i + 1)
                    if not (isinstance(k, int) and k == 0 and i < NLO):
                        pool.wait_ge(S("w_used"), 2 * NPC * k + i - NLO + 1)
                    if not (isinstance(k, int) and k == 0 and i == 0):
                        pool.wait_ge(S("lo_ready"), 2 * NPC * k + i)
                    g.tensor_tensor(wlo[i % NLO][:, 3, :], w32[i % NW][:, 3, :], whi[i % NHI][:, 3, :].bitcast(F32),
                                    ALU.subtract).then_inc(S("lo_pool"), 1)
            pair(0)
            with pool.Fori(1, NPAIR) as k:
                pair(k)
            pool.wait_ge(S("flag_ready"), 1)
            over_ = pool.value_load(flagi[0:1, 0:1], min_val=0, max_val=1)
            with pool.If(over_ > 0):
                with pool.Fori(NPAIR, NPAIR * NBLK) as k:
                    pair(k)
            pool.nop()
            pool.wait_ge(S("shift_out"), 16 * (NS + 1))
            pool.wait_ge(S("prompt_state_out"), 16)
            pool.wait_ge(S("rwkv_out"), 128)

        @block.tensor
        def _(pe):
            mm = nc.tensor.matmul

            def free(stage, i):
                n_ = UPOS[stage, i]
                if BEFORE[n_] is not None:
                    s, k = UNITS[BEFORE[n_]]
                    pe.wait_ge(S(f"{s}_ready"), k + 1)
                return banks[BANK[n_]]

            def filled(ins, stage):
                ins.then_inc(S("unit_filled"), 1)

            pe.wait_ge(S("ident_ready"), 1)
            pe.wait_ge(S("prow_in"), 16 * 11)
            b = free("params", 0)
            filled(nc.tensor.transpose(b[:, 0:NPAR], prow[0:NPAR, :], ident[0:NPAR, 0:NPAR]), "params")
            pe.wait_ge(S("h_done"), 3)
            pe.wait_ge(S("x_in"), 64)
            for c in range(KT):
                b = free("hT", c)
                for tile in range(3):
                    tn = 72 if tile == 2 else P
                    last = nc.tensor.transpose(b[:, P * tile:P * tile + tn], h[0:tn, tile, P * c:P * c + P],
                                               ident[0:tn, 0:tn])
                filled(last, "hT")

            def proj(n0, n1):
                for n_ in range(n0, n1):
                    j, chunk, k = PROJ[n_]
                    pe.wait_ge(S(f"ring{chunk % 6}"), 16 * (chunk // 6 + 1))
                    pe.wait_ge(S("hT_ready"), KT)
                    b_ = free("proj", n_)
                    w = slot(chunk % 6).rearrange("p (c n) -> p c n", c=KT)
                    nn = NTP if j >= 16 else NT
                    for c in range(KT):
                        last_ = mm(b_[:, 0:nn], w[:, c, P * k:P * k + P], hT[:, c, 0:nn], start=(c == 0), stop=(c == KT - 1))
                    filled(last_, "proj")
            proj(0, 14)
            pe.wait_ge(S("lora_in"), 48)
            for j in range(4):
                pe.wait_ge(S("lora_act"), 1)
                b = free("wpre", j)
                filled(mm(b[:, 0:NT], w2a2[0:64, P * j:P * j + P], lor[0:64, 0, :], start=True, stop=True), "wpre")
            for j in range(4):
                b = free("apre", j)
                filled(mm(b[:, 0:NT], w2a2[64:128, P * j:P * j + P], lor[64:128, 0, :], start=True, stop=True), "apre")
            for j in range(4):
                pe.wait_ge(S("lora_act"), 2)
                b = free("gpre", j)
                filled(mm(b[:, 0:NT], g2w[:, P * j:P * j + P], lor[:, 1, :], start=True, stop=True), "gpre")
            proj(14, 22)

            def head_sums(stage, src, ready, count):
                pe.wait_ge(S(ready), count)
                b_ = free(stage, 0)
                for tile in range(3):
                    for j in range(4):
                        o = 8 * tile + 2 * j
                        last_ = mm(b_[0:TN[tile], o:o + 2], src[:, j, TOFF[tile]:TOFF[tile] + TN[tile]], blk[:, 0:65:64],
                                   start=True, stop=True)
                filled(last_, stage)

            def head_spread(stage, col, ready):
                pe.wait_ge(S(ready), 1)
                for j in range(4):
                    b_ = free(stage, j)
                    for tile in range(3):
                        tn = TN[tile]
                        for p_ in range(2):
                            src = nrm[0:tn, col, 8 * tile + 2 * j + p_:8 * tile + 2 * j + p_ + 1].broadcast_to([tn, RN])
                            last_ = mm(b_[64 * p_:64 * p_ + 64, TOFF[tile]:TOFF[tile] + tn], src, ident[0:tn, 0:tn],
                                       start=True, stop=True)
                    filled(last_, stage)
            head_sums("kss", tB, "ksq", 4)
            proj(22, 26)
            head_spread("knb", 1, "kinv_ready")
            proj(26, len(PROJ) - LATE)
            pe.wait_ge(S("proj_ready"), 26)
            for tile in range(3):
                b = free("itok", tile)
                for j in range(4):
                    last = nc.tensor.transpose(b[0:TN[tile], P * j:P * j + P], hi[:, j, TOFF[tile]:TOFF[tile] + TN[tile]],
                                               ident[:, :])
                filled(last, "itok")
            at = 0
            for i, hh in enumerate(LEVELS + [0]):
                if hh:
                    pe.wait_ge(S("qp_ready"), i + 1)
                    if i:
                        pe.wait_ge(S("ks_ready"), i)
                for tile in range(3 if hh <= 4 else 2):
                    tn, to = TN[tile], TOFF[tile]
                    b = free("lvl", at)
                    kk_ = ks if i and hh else hk
                    qq = qp if hh else hq
                    for j in range(4):
                        last = mm(b[0:tn, tn * j:tn * j + tn], kk_[:, j, to:to + tn], qq[:, j, to:to + tn], start=True, stop=True)
                    filled(last, "lvl")
                    at += 1
                if i < LATE:
                    proj(len(PROJ) - LATE + i, len(PROJ) - LATE + i + 1)
            pe.wait_ge(S("ks_ready"), len(LEVELS))
            for tile in range(3):
                b = free("kstok", tile)
                for j in range(4):
                    last = nc.tensor.transpose(b[0:TN[tile], P * j:P * j + P], ks[:, j, TOFF[tile]:TOFF[tile] + TN[tile]],
                                               ident[:, :])
                filled(last, "kstok")

            def at_tile(tile):
                tn = TN[tile]
                return at_[0:tn, 512 * tile:512 * tile + 4 * tn].rearrange("p (j t) -> p j t", t=tn)

            def hstate(stage, tile):
                b_ = free(stage, 0)
                for j in range(4):
                    last_ = mm(b_[:, P * j:P * j + P], kstok[:, tile, P * j:P * j + P], itok[:, tile, P * j:P * j + P],
                               start=True, stop=True)
                filled(last_, stage)
            pe.wait_ge(S("kstok_ready"), 3)
            pe.wait_ge(S("itok_ready"), 3)
            hstate("hs1", 0)
            pe.wait_ge(S("at_ready"), 1)
            pe.wait_ge(S("qp_ready"), 8)
            for tile in range(3):
                tn, to = TN[tile], TOFF[tile]
                b = free("ho", tile)
                if tile == 1:
                    pe.wait_ge(S("hs1_ready"), 1)
                if tile == 2:
                    pe.wait_ge(S("hs0_in"), 16)
                for j in range(4):
                    o = b[:, tn * j:tn * j + tn]
                    last = mm(o, itok[0:tn, tile, P * j:P * j + P], at_tile(tile)[:, j, :], start=True, stop=(tile == 0),
                              skip_group_check=True)
                    if tile == 1:
                        last = mm(o, hs[:, j, :], qp[:, j, to:to + tn], start=False, stop=True, skip_group_check=True)
                    if tile == 2:
                        for q in range(NS):
                            last = mm(o[:, TS * q:TS * q + TS], hs0[:, q, j, :], qp[:, j, to + TS * q:to + TS * q + TS],
                                      start=False, stop=(q == NS - 1), skip_group_check=True)
                filled(last, "ho")
            hstate("hs2", 1)
            for j in range(HGH):
                pe.wait_ge(S("imask_ready"), j + 1)
                for half in range(2):
                    b = free("hsend", 2 * j + half)
                    filled(mm(b[:, :], kstok[0:64, 2, P * j:P * j + P],
                              imask[0:64, j % 2, 4 * half:4 * half + 4, :].rearrange("p b v -> p (b v)"),
                              start=True, stop=True), "hsend")
            pe.wait_ge(S("osq"), 1)
            b = free("hvar", 0)
            for tile in range(3):
                for j in range(4):
                    last = mm(b[0:TN[tile], 4 * tile + j:4 * tile + j + 1], hi[:, j, TOFF[tile]:TOFF[tile] + TN[tile]],
                              ones[:, 0:1], start=True, stop=True)
            filled(last, "hvar")
            pe.wait_ge(S("oinv_ready"), 1)
            for j in range(4):
                b = free("hvarb", j)
                for tile in range(3):
                    tn = TN[tile]
                    last = nc.tensor.transpose(b[:, TOFF[tile]:TOFF[tile] + tn],
                                               nrm[0:tn, 2, 4 * tile + j:4 * tile + j + 1].broadcast_to([tn, P]),
                                               ident[0:tn, 0:tn])
                filled(last, "hvarb")
            pe.wait_ge(S("rbon_in"), 4)
            for j in range(4):
                b = free("bonus", j)
                filled(mm(b[:, 0:NT], blk[:, :], rbon[:, j, :], start=True, stop=True), "bonus")
            pe.wait_ge(S("s0_in"), 128)
            for q in range(4):
                b = free("s0t", q)
                for j in range(4):
                    last = nc.tensor.transpose(b[:, P * j:P * j + P],
                                               s0raw[:, q, 2 * j:2 * j + 2, :].rearrange("p h k -> p (h k)"), ident[:, :])
                filled(last, "s0t")

            def tokens(stage, src):
                for tile_ in range(3):
                    tn_, b_ = TN[tile_], free(stage, tile_)
                    for j_ in range(4):
                        last_ = nc.tensor.transpose(b_[0:tn_, P * j_:P * j_ + P], src[:, j_, TOFF[tile_]:TOFF[tile_] + tn_],
                                                    ident[:, :])
                    filled(last_, stage)
            pe.wait_ge(S("rw_ready"), 1)
            tokens("vtok", rv)
            tokens("btok", ra)
            tokens("ktok", rk)

            def gram(stage, lhs, rhs):
                for tile_ in range(3):
                    tn_, to_ = TN[tile_], TOFF[tile_]
                    for p_ in range(2):
                        b_ = free(stage, 2 * tile_ + p_)
                        rows = slice(64 * p_, 64 * p_ + 64)
                        for j_ in range(4):
                            last_ = mm(b_[0:tn_, tn_ * j_:tn_ * j_ + tn_], lhs[rows, j_, to_:to_ + tn_],
                                       rhs[rows, j_, to_:to_ + tn_], start=True, stop=True)
                        filled(last_, stage)
            gram("gM", rkk, ra)
            gram("gN", ra, rkk)
            gram("gK", rk, rkk)
            gram("gRb", ra, rr)
            gram("gRk", rk, rr)
            done = {"mZ": 0, "mW": 0, "mT": 0}
            for i, hh in enumerate(LEVELS):
                if hh == 1:
                    continue
                units = [(tile, p) for tile in range(3 if hh <= 4 else 2) for p in range(2)]
                for stage, lhs, rhs in (("mZ", mM_, mW_), ("mW", mT_, mZ_), ("mT", mZ_, mT_)):
                    if stage == "mT" and hh == 64:
                        continue
                    for x, (tile, p) in enumerate(units):
                        tn, k = TN[tile], done[stage]
                        if stage == "mZ":
                            pe.wait_ge(S("gM_ready"), 6)
                            if hh == 2:
                                pe.wait_ge(S("gN_ready"), x + 1)
                            else:
                                pe.wait_ge(S("mW_ready"), done["mW"] - (6 if hh <= 8 else 4) + x + 1)
                        else:
                            pe.wait_ge(S("mZ_ready"), done["mZ"] - len(units) + x + 1)
                            if hh == 2:
                                pe.wait_ge(S("T1_ready"), x + 1)
                            elif stage == "mW":
                                pe.wait_ge(S("mT_ready"), done["mT"] - (6 if hh <= 8 else 4) + x + 1)
                        b = free(stage, k)
                        for j in range(4):
                            last = mm(b[0:tn, tn * j:tn * j + tn], lhs(tile, p)[:, j, :], rhs(tile, p)[:, j, :],
                                      start=True, stop=True)
                        filled(last, stage)
                        done[stage] += 1
            pe.wait_ge(S("s0t_ready"), 4)
            for p in range(2):
                b = free("rst", p)
                rows = slice(64 * p, 64 * p + 64)
                for j in range(4):
                    for q in range(NS):
                        o = 64 * j + TS * q
                        last = mm(b[rows, o:o + TS], s0t[rows, q // 2, j, q % 2, :], rkk[rows, j, NP_ + TS * q:NP_ + TS * q + TS],
                                  start=True, stop=True)
                filled(last, "rst")
            pe.wait_ge(S("mW_ready"), 28)
            pe.wait_ge(S("vtok_ready"), 3)
            pe.wait_ge(S("btok_ready"), 3)
            pe.wait_ge(S("ktok_ready"), 3)
            for tile in range(3):
                tn, to = TN[tile], TOFF[tile]
                if tile == 1:
                    pe.wait_ge(S("S_ready"), 2)
                if tile == 2:
                    pe.wait_ge(S("rst_ready"), 2)
                for p in range(2):
                    rows = slice(64 * p, 64 * p + 64)
                    b = free("R", 2 * tile + p)
                    for j in range(4):
                        hd = slice(P * j + 64 * p, P * j + 64 * p + 64)
                        o = b[0:tn, 64 * j:64 * j + 64]
                        last = mm(o, mK_(tile, p)[:, j, :], vtok[0:tn, tile, hd], start=True, stop=(tile == 0))
                        if tile == 1:
                            last = mm(o, rkk[rows, j, to:to + tn], sp[rows, 64 * j:64 * j + 64], start=False, stop=True)
                        if tile == 2:
                            last = mm(o, rst[:, j, :], ident[:, rows], start=False, stop=True)
                    filled(last, "R")
                for p in range(2):
                    pe.wait_ge(S("R_ready"), 2 * tile + p + 1)
                    b = free("U", 2 * tile + p)
                    for j in range(4):
                        hd = slice(P * j + 64 * p, P * j + 64 * p + 64)
                        last = mm(b[0:tn, 64 * j:64 * j + 64], mW_(tile, p)[:, j, :], rR[0:tn, tile, hd], start=True, stop=True)
                    filled(last, "U")
                for p in range(2):
                    pe.wait_ge(S("U_ready"), 2 * tile + p + 1)
                    rows = slice(64 * p, 64 * p + 64)
                    b = free("Y", 2 * tile + p)
                    for j in range(4):
                        hd = slice(P * j + 64 * p, P * j + 64 * p + 64)
                        o = b[rows, tn * j:tn * j + tn]
                        mm(o, uu[0:tn, tile, hd], mRb_(tile, p)[:, j, :], start=(tile < 2 or j == 0), stop=False,
                           skip_group_check=True)
                        last = mm(o, vtok[0:tn, tile, hd], mRk_(tile, p)[:, j, :], start=False, stop=(tile == 0),
                                  skip_group_check=True)
                        if tile == 1:
                            last = mm(o, sp[rows, 64 * j:64 * j + 64], rr[rows, j, to:to + tn], start=False, stop=True,
                                      skip_group_check=True)
                    if tile == 2:
                        last.then_inc(S("y_half"), 1)
                        pe.wait_ge(S("y_half"), p + 1)
                        for j in range(4):
                            o = b[rows, tn * j:tn * j + tn]
                            for q in range(NS):
                                t0 = NP_ + TS * q
                                last = mm(o[:, TS * q:TS * q + TS], s0t[rows, q // 2, j, q % 2, :], rr[rows, j, t0:t0 + TS],
                                          start=False, stop=(q == NS - 1), skip_group_check=True)
                    filled(last, "Y")
                if tile < 2:
                    for p in range(2):
                        rows = slice(64 * p, 64 * p + 64)
                        b = free("S", 2 * tile + p)
                        for j in range(4):
                            hd = slice(P * j + 64 * p, P * j + 64 * p + 64)
                            o = b[rows, 64 * j:64 * j + 64]
                            mm(o, btok[:, tile, hd], uu[:, tile, hd], start=True, stop=False)
                            last = mm(o, ktok[:, tile, hd], vtok[:, tile, hd], start=False, stop=True)
                        filled(last, "S")
            early = [(x, c) for x in range(4) for c in range(4)]

            def output_early(n_):
                for _ in range(min(n_, len(early))):
                    x, c = early.pop(0)
                    if c == 0:
                        free("xo", x)
                    tn_, to_ = TN[x // 2], TOFF[x // 2]
                    mm(bank("xo", x)[0:tn_, :], hq[:, c, to_:to_ + tn_], slot(0)[:, c * DM + 512 * (x % 2):c * DM + 512 * (x % 2) + 512],
                       start=(c == 0), stop=False)
            pe.wait_ge(S("mix_hg"), 1)
            pe.wait_ge(S("ring0"), 48)
            for j in range(4):
                b = free("send", j)
                for p in range(2):
                    x = 2 * j + p
                    hd = slice(P * j + 64 * p, P * j + 64 * p + 64)
                    pe.wait_ge(S("um_ready"), x + 1)
                    pe.wait_ge(S("vm_ready"), x + 1)
                    o = b[64 * p:64 * p + 64, :]
                    mm(o, btok[0:64, 2, hd], um[0:64, x % 2].rearrange("p b v -> p (b v)"), start=True, stop=False)
                    last = mm(o, ktok[0:64, 2, hd], vm[0:64, x % 2].rearrange("p b v -> p (b v)"), start=False, stop=True)
                    if p == 0:
                        last.then_inc(S("send_half"), 1)
                filled(last, "send")
                output_early(EARLY[0])
            pe.wait_ge(S("S_ready"), 4)
            b = free("pst", 0)
            for j in range(4):
                last = nc.tensor.transpose(b[0:64, P * j:P * j + P], sp[:, 64 * j:64 * j + 64], ident[:, :])
            filled(last, "pst")
            output_early(EARLY[1])
            pe.wait_ge(S("send_ready"), 4)
            for q in range(4):
                b = free("sout", q)
                for j in range(4):
                    last = nc.tensor.transpose(b[:, P * j:P * j + P], s0t[:, q, j].rearrange("p c v -> p (c v)"), ident[:, :])
                filled(last, "sout")
            pe.wait_ge(S("Y_ready"), 6)
            for j in range(4):
                b = free("mean", j)
                filled(mm(b[:, 0:NT], blkm[:, :], yy[:, j, :], start=True, stop=True), "mean")
            output_early(EARLY[2])
            head_sums("var", ra, "ysq", 4)
            output_early(EARLY[3])
            head_spread("varb", 3, "yinv_ready")
            output_early(len(early))
            pe.wait_ge(S("mixer_done"), 1)
            pe.wait_ge(S("ring1"), 48)
            for tile in range(3):
                for half in range(2):
                    x = 2 * tile + half
                    b = free("xo", x) if x >= 4 else bank("xo", x)
                    tn, to = TN[tile], TOFF[tile]
                    for c in range(4 if x < 4 else 0, KT):
                        lhs = (hq if c < 4 else yy)[:, c % 4, to:to + tn]
                        o = (c % 4) * DM + 512 * half
                        last = mm(b[0:tn, :], lhs, slot(c // 4)[:, o:o + 512], start=(c == 0), stop=(c == KT - 1))
                    filled(last, "xo")
            pe.wait_ge(S("brow_in"), 32)
            b = free("bias", 0)
            for a in range(4):
                last = nc.tensor.transpose(b[:, P * a:P * a + P], brows[:, a, :], ident[:, :])
            filled(last, "bias")
            for tile in range(3):
                tn = TN[tile]
                pe.wait_ge(S("h2_done"), tile + 1)
                for c in range(KT):
                    b = free("h2T", c) if tile == 0 else bank("h2T", c)
                    last = nc.tensor.transpose(b[:, P * tile:P * tile + tn], h2[0:tn, tile, P * c:P * c + P], ident[0:tn, 0:tn])
                    if tile == 2:
                        filled(last, "h2T")
            pe.wait_ge(S("h2T_ready"), KT)
            pe.wait_ge(S("router_in"), 32)
            b = free("logit", 0)
            for tile in range(3):
                for c in range(KT):
                    last = mm(b[0:TN[tile], NE * tile:NE * tile + NE], hT[:, c, TOFF[tile]:TOFF[tile] + TN[tile]], wr[:, c, :],
                              start=(c == 0), stop=(c == KT - 1))
            filled(last, "logit")
            pe.wait_ge(S("msk_ready"), 3)
            b = free("rank", 0)
            for tile in range(3):
                tn = TN[tile]
                for e_ in range(tile):
                    mm(b[0:tn, NE * tile:NE * tile + NE], ones[:, 0:tn], msk[:, e_, :], start=(e_ == 0), stop=False)
                mm(b[0:tn, NE * tile:NE * tile + NE], strict[0:tn, 0:tn], msk[0:tn, tile, :], start=(tile == 0), stop=True)
            for tile in range(3):
                tn = TN[tile]
                last = mm(b[0:1, 96:96 + NE], ones[0:tn, 0:1], msk[0:tn, tile, :], start=(tile == 0), stop=(tile == 2))
            filled(last, "rank")
            b = free("gT", 0)
            for tile in range(3):
                tn = TN[tile]
                last = nc.tensor.transpose(b[0:NE, TOFF[tile]:TOFF[tile] + tn], gate[0:tn, tile, 0:NE], ident[0:tn, 0:tn])
            filled(last, "gT")

            stream, bG, bU, bX, bY = banks[0:2], banks[2], banks[3], banks[4:6], banks[6:8]

            def gather(k, half):
                pe.wait_ge(S("sel_ready"), k + 1)
                for c in range(4 * half, 4 * half + 4):
                    for tile_ in range(3):
                        tn_ = TN[tile_]
                        last_ = mm(bX[c // 4][:, P * (c % 4):P * (c % 4) + P], h2[0:tn_, tile_, P * c:P * c + P],
                                   sel[0:tn_, tile_, :], start=(tile_ == 0), stop=(tile_ == 2))
                last_.then_inc(S("gathered"), 1)

            def product(e, i, lhs):
                j = (i % NPC) // 2
                pe.wait_ge(S("lo_ready"), e * NPC + i % NPC + 1)
                pe.wait_ge(S("lo_pool"), e * NPC + i % NPC + 1)
                if i % 2 == 0 and not (isinstance(e, int) and e * NG + j < 2):
                    pe.wait_ge(S("group_read"), e * NG + j - 1)
                for q in range(4):
                    c = 4 * (i % 2) + q
                    mm(stream[j % 2][:, :], lhs(c), whi[i % NHI][:, q, :],
                       start=(c == 0), stop=False)
                    last_ = mm(stream[j % 2][:, :], lhs(c), wlo[i % NLO][:, q, :],
                               start=False, stop=(c == KT - 1))
                last_.then_inc(S("w_used"), 1)

            def combine(e, j):
                pe.wait_ge(S("group_read"), e * NG + j + 1)
                pe.wait_ge(S("gu_read"), 2 * e)
                for q in range(4):
                    o = CAP * (4 * (j // 2) + q)
                    last_ = mm((bG, bU)[j % 2][:, o:o + CAP], gup[:, j % 2, P * q:P * q + P], twin[:, :], start=True, stop=True)
                last_.then_inc(S("combined"), 1)

            def turn(e):
                pe.wait_ge(S("selg_ready"), e + 1)
                pe.wait_ge(S("acc_added"), 8 * e)
                for tile_ in range(3):
                    tn_ = TN[tile_]
                    last_ = nc.tensor.transpose(bY[0][:, TOFF[tile_]:TOFF[tile_] + tn_],
                                                selg[0:tn_, tile_, :, :].rearrange("p n s -> p (n s)"), ident[0:tn_, 0:tn_])
                last_.then_inc(S("selg_turned"), 1)

            def scatter(e, c0):
                if c0 == 0:
                    pe.wait_ge(S("scat_ready"), e + 1)
                    pe.wait_ge(S("group_read"), (e + 1) * NG)
                for c in (c0, c0 + 1):
                    if c:
                        pe.wait_ge(S("acc_added"), 8 * e + c - 1)
                    mm(bY[c % 2][:, 0:NT], ytk[:, P * c:P * c + P], scat[:, :], start=True, stop=True)\
                        .then_inc(S("scattered"), 1)

            def pair(k, before):
                for ab in range(2):
                    e = k * 2 + ab

                    def tokens_(c):
                        return xg[:, c, ab, :, :].rearrange("p n s -> p (n s)")

                    def hidden(c):
                        return h1b[:, P * c:P * c + P]
                    for i in range(2 * len(GROUPS)):
                        if i == 0 and ab == 0:
                            pe.wait_ge(S("xg_ready"), k + 1)
                        product(e, NPC * ab + i, tokens_)
                        if i in (2, 4, 6):
                            combine(e, i // 2 - 1)
                        if before or ab:
                            if i == 0:
                                turn(e - 1)
                            if i >= 5:
                                scatter(e - 1, 2 * (i - 5))
                    gather(k + 1, ab)
                    combine(e, 3)
                    if before or ab:
                        scatter(e - 1, 6)
                    for i in range(2 * len(GROUPS), NPC):
                        pe.wait_ge(S("h1_ready"), 2 * e + i % 2 + 1)
                        product(e, NPC * ab + i, hidden)

            def finish(e):
                turn(e)
                for c0 in range(0, KT, 2):
                    scatter(e, c0)
            for s, k in (("h2T", KT), ("logit", 1), ("rank", 1), ("bias", 1), ("gT", 1)):
                pe.wait_ge(S(f"{s}_ready"), k)
            gather(0, 0)
            gather(0, 1)
            for c in range(KT):
                if c >= len(BIAS_BANKS):
                    pe.wait_ge(S("accb_ready"), c - len(BIAS_BANKS) + 1)
                mm(banks[BIAS_BANKS[c % len(BIAS_BANKS)]][:, 0:NT], bdr[:, P * c:P * c + P], gateT[:, :],
                   start=True, stop=True).then_inc(S("accb_done"), 1)
            pe.wait_ge(S("accb_ready"), KT)
            pe.wait_ge(S("twin_ready"), 1)

            def blocks(k0, k1):
                pair(k0, False)
                with pe.Fori(k0 + 1, k1 - 1) as k:
                    pair(k, True)
                pair(k1 - 1, True)
                finish(2 * k1 - 1)
            blocks(0, NPAIR)
            pe.wait_ge(S("flag_ready"), 1)
            over_ = pe.value_load(flagi[0:1, 0:1], min_val=0, max_val=1)
            with pe.If(over_ > 0):
                blocks(NPAIR, NPAIR * NBLK)
            pe.nop()
            pe.wait_ge(S("acc_done"), 1)
            for tile in range(3):
                tn, to = TN[tile], TOFF[tile]
                for c in range(KT):
                    last = nc.tensor.transpose(banks[2 * tile + c // 4][0:tn, P * (c % 4):P * (c % 4) + P],
                                               acc[:, c, to:to + tn], ident[:, :])
                last.then_inc(S("acc_turned"), 1)

        @block.scalar
        def _(act):
            a = nc.scalar.activation
            cp = nc.scalar.copy

            def wait_filled(stage, i):
                act.wait_ge(S("unit_filled"), U(stage, i + 1))
                return bank(stage, i)

            def ready(ins, stage):
                ins.then_inc(S(f"{stage}_ready"), 1)

            def norms(k, src, name):
                for tile_ in range(3):
                    r_, o_ = TN[tile_], st[0:TN[tile_], 3 * k + tile_:3 * k + tile_ + 1]
                    if name:
                        act.wait_ge(S(name), 2 * tile_ + 2)
                    a(junk[0:r_, :], src[0:r_, tile_, :], ACT.Square, accum_out=o_).then_inc(S("ssq"), 1)
                    act.wait_ge(S("ssq"), 3 * k + tile_ + 1)
                    a(o_, o_, ACT.Sqrt, scale=1.0 / DM, bias=epst[0:r_, 0:1]).then_inc(S("rms"), 1)
            act.wait_ge(S("x_in"), 64)
            act.wait_ge(S("ident_ready"), 1)
            norms(0, h, None)
            act.wait_ge(S("par_ready"), 1)
            a(der[:, 0:4], der[:, 0:4], ACT.Sigmoid).then_inc(S("lb_ready"), 1)
            nraw = 0
            for n, (j, _, _) in enumerate(PROJ):
                if n == len(PROJ) - LATE:
                    for tile in range(3):
                        tn = TN[tile]
                        ready(cp(itok[0:tn, tile, :], wait_filled("itok", tile)[0:tn, :]), "itok")
                b = wait_filled("proj", n)
                if 12 <= j < 16 or j < 4:
                    if n >= 2:
                        act.wait_ge(S("raw_used"), nraw - 1)
                    dst = hq if j < 4 else hg
                    a(dst[:, j % 4, :], b[:, 0:NT], ACT.Sigmoid)
                    ready(cp(raw[:, nraw % 2, 0:NT], b[:, 0:NT]), "proj")
                    nraw += 1
                elif j < 8:
                    ready(a(hf[:, j - 4, :], b[:, 0:NT], ACT.Sigmoid), "proj")
                elif j < 12:
                    ready(cp(hi[:, j - 8, :], b[:, 0:NT]), "proj")
                else:
                    if nraw >= 2:
                        act.wait_ge(S("raw_used"), nraw - 1)
                    ready(cp(raw[:, nraw % 2, :], b[:, 0:NTP]), "proj")
                    nraw += 1
                if j == 29:
                    act.wait_ge(S("lor_ready"), 2)
                    a(lor[0:64, 0, :], lor[0:64, 0, :], ACT.Tanh).then_inc(S("lora_act"), 1)
                    a(lor[:, 1, :], lor[:, 1, :], ACT.Sigmoid).then_inc(S("lora_act"), 1)
                if n == 13:
                    for j2 in range(4):
                        ready(a(rs[:, j2, :], wait_filled("wpre", j2)[:, 0:NT], ACT.Sigmoid, bias=pcol("w0", j2)), "wpre")
                    for j2 in range(4):
                        ready(a(ra[:, j2, :], wait_filled("apre", j2)[:, 0:NT], ACT.Sigmoid, bias=pcol("a0", j2)), "apre")
                    for j2 in range(4):
                        ready(cp(rg[:, j2, :], wait_filled("gpre", j2)[:, 0:NT]), "gpre")
                    act.wait_ge(S("mixed"), 14)
                    act.wait_ge(S("hT_ready"), KT)
                    for j2 in range(4):
                        a(tB[:, j2, :], rk[:, j2, :], ACT.Square, scale=pcol("kk", j2)).then_inc(S("ksq"), 1)
                if n == 21:
                    b = wait_filled("kss", 0)
                    a(nrm[:, 0, 0:16], b[:, 0:16], ACT.Sqrt)
                    ready(a(nrm[0:64, 0, 16:24], b[0:64, 16:24], ACT.Sqrt), "kss")
                if n == 25:
                    act.wait_ge(S("cen_ready"), 1)
                    a(ec[:, 0:4], cen[:, 1, :], ACT.Exp, scale=-EDEC)
                    act.wait_ge(S("gs_ready"), 1)
                    act.wait_ge(S("unit_filled"), U("kss", 1))
                    a(tB[:, :, :], tA[:, :, :], ACT.Exp, scale=EDEC).then_inc(S("e2_ready"), 1)
                    a(rs[:, :, :], rs[:, :, :], ACT.Exp, scale=-EDEC).then_inc(S("e3_ready"), 1)
                    act.wait_ge(S("e2_ready"), 1)
                    a(tA[:, :, :], tA[:, :, :], ACT.Exp, scale=-EDEC).then_inc(S("e1_ready"), 1)
            for tile in range(3):
                tn = TN[tile]
                ready(cp(kstok[0:tn, tile, :], wait_filled("kstok", tile)[0:tn, :]), "kstok")
            ready(cp(hs[:, :, :], wait_filled("hs1", 0)[:, :].rearrange("p (h v) -> p h v", v=P)), "hs1")
            for tile in range(3):
                tn, to = TN[tile], TOFF[tile]
                src = wait_filled("ho", tile)[:, 0:4 * tn].rearrange("p (j t) -> p j t", t=tn)
                ready(cp(hq[:, :, to:to + tn], src), "ho")
            act.wait_ge(S("ho_ready"), 3)
            a(hi[:, :, :], hq[:, :, :], ACT.Square).then_inc(S("osq"), 1)
            b = wait_filled("hvar", 0)
            a(nrm[:, 2, 0:8], b[:, 0:8], ACT.Sqrt, scale=1.0 / P, bias=epst[:, 0:1])
            ready(a(nrm[0:64, 2, 8:12], b[0:64, 8:12], ACT.Sqrt, scale=1.0 / P, bias=epst[0:64, 0:1]), "hvar")
            act.wait_ge(S("mix_hg"), 1)
            for q in range(4):
                ready(cp(s0t[:, q].rearrange("p j c v -> p j (c v)"),
                         wait_filled("s0t", q)[:, :].rearrange("p (j x) -> p j x", j=4)), "s0t")
            for stage, dst in (("vtok", vtok), ("btok", btok), ("ktok", ktok)):
                for tile in range(3):
                    tn = TN[tile]
                    b = wait_filled(stage, tile)
                    if stage == "vtok":
                        act.wait_ge(S("unit_filled"), U("s0t", 4))
                    ready(cp(dst[0:tn, tile, :], b[0:tn, :]), stage)
            act.wait_ge(S("hgrn_out"), 32)
            act.wait_ge(S("mix_hg"), 1)
            for x in range(6):
                tn = TN[x // 2]
                ready(cp(mM_(x // 2, x % 2), wait_filled("gM", x)[0:tn, 0:4 * tn].rearrange("p (j t) -> p j t", t=tn)), "gM")
            act.wait_ge(S("unit_filled"), U("mZ", 28))
            act.wait_ge(S("unit_filled"), U("mW", 28))
            for p in range(2):
                b = wait_filled("rst", p)
                rows = slice(64 * p, 64 * p + 64)
                ready(cp(rst[rows, :, :], b[rows, 0:256].rearrange("p (j t) -> p j t", t=64)), "rst")
            for tile in range(3):
                tn, to = TN[tile], TOFF[tile]
                for stage, dst in (("R", rR), ("U", uu)):
                    for p in range(2):
                        b = wait_filled(stage, 2 * tile + p)
                        o = dst[0:tn, tile, :].rearrange("p (j c v) -> p j c v", c=2, v=RN)[:, :, p, :]
                        ready(cp(o, b[0:tn, 0:256].rearrange("p (j v) -> p j v", v=RN)), stage)
                for p in range(2):
                    rows = slice(64 * p, 64 * p + 64)
                    b = wait_filled("Y", 2 * tile + p)
                    ready(cp(yy[rows, :, to:to + tn], b[rows, 0:4 * tn].rearrange("p (j t) -> p j t", t=tn)), "Y")
            ready(cp(pout[:, :], wait_filled("pst", 0)[0:64, :]), "pst")
            for q in range(4):
                ready(cp(sout[:, q].rearrange("p j k -> p (j k)"), wait_filled("sout", q)[:, :]), "sout")
            act.wait_ge(S("yc_ready"), 4)
            for j in range(4):
                a(ra[:, j, :], yy[:, j, :], ACT.Square).then_inc(S("ysq"), 1)
            b = wait_filled("var", 0)
            a(nrm[:, 2, 0:16], b[:, 0:16], ACT.Sqrt, scale=1.0 / RN, bias=epst[:, 1:2])
            ready(a(nrm[0:64, 2, 16:24], b[0:64, 16:24], ACT.Sqrt, scale=1.0 / RN, bias=epst[0:64, 1:2]), "var")
            act.wait_ge(S("unit_filled"), U("bias", 1))
            ready(cp(bgu[:, :], bank("bias", 0)[:, :]), "bias")
            norms(1, h, "xo_ready")
            act.wait_ge(S("top_ready"), 3)
            for tile in range(3):
                tn = TN[tile]
                a(gat[0:tn, tile, 0:4], gat[0:tn, tile, 0:4], ACT.Exp).then_inc(S("top_exp"), 1)

            ready(cp(gateT[:, :], wait_filled("gT", 0)[0:NE, 0:NT]), "gT")

            def high(k, i):
                q = 2 * NPC * k + i
                act.wait_ge(S(f"w{i % NW}_in"), 16 * (2 * NPC // NW * k + i // NW + 1))
                if not (isinstance(q, int) and q < NHI):
                    act.wait_ge(S("w_used"), q - NHI + 1)
                cp(whi[i % NHI], w32[i % NW]).then_inc(S("hi_ready"), 1)

            def tokens_high(k):
                for i in range(2):
                    act.wait_ge(S("gathered"), 2 * k + i + 1)
                    for ab in range(2):
                        b_ = banks[4 + i][:, :].rearrange("p (c b s) -> p c b s", b=2, s=CAP)[:, :, ab, :]
                        last_ = cp(xg[:, 4 * i:4 * i + 4, ab, 0, :], b_)
                last_.then_inc(S("xg_high"), 1)

            def group_out(e, j):
                act.wait_ge(S("w_used"), e * NPC + 2 * j + 2)
                if j < len(GROUPS):
                    if not (isinstance(e, int) and e * 4 + j < 2):
                        act.wait_ge(S("combined"), e * 4 + j - 1)
                    dst = gup[:, j % 2, :]
                else:
                    act.wait_ge(S("scattered"), 8 * e)
                    dst = ytk[:, NCOL * (j - 4):NCOL * (j - 3)]
                cp(dst, banks[j % 2][:, :]).then_inc(S("group_read"), 1)

            def sigmoid(e, i):
                act.wait_ge(S("gate_ready"), 2 * e + i + 1)
                a(sg[:, 4 * i:4 * i + 4, :], gg[:, 4 * i:4 * i + 4, :], ACT.Sigmoid, scale=ALPHA).then_inc(S("sig_ready"), 1)

            def gates_out(e):
                act.wait_ge(S("selg_turned"), e + 1)
                act.wait_ge(S("scattered"), 8 * e)
                cp(scat[:, :], banks[6][:, 0:NT]).then_inc(S("scat_ready"), 1)

            def pair(k, before, last):
                for ab in range(2):
                    e = k * 2 + ab
                    for i in range(NPC):
                        if (before or ab) and i == 0:
                            group_out(e - 1, NG - 1)
                        if (before or ab) and i == 1:
                            gates_out(e - 1)
                        if i in (2, 4, 6, 8, 10):
                            group_out(e, i // 2 - 1)
                        if i == 5:
                            sigmoid(e, 0)
                        if i == 9 and ab:
                            tokens_high(k + 1)
                        ahead = NPC * ab + i + NHI - 1
                        if not last or ahead < 2 * NPC:
                            high(k, ahead)
                        if i == 8:
                            sigmoid(e, 1)

            def blocks(k0, k1):
                if k0:
                    for i in range(NHI - 1):
                        high(k0, i)
                pair(k0, False, False)
                with act.Fori(k0 + 1, k1 - 1) as k:
                    pair(k, True, False)
                pair(k1 - 1, True, True)
                group_out(2 * k1 - 1, NG - 1)
                gates_out(2 * k1 - 1)
            high(0, 0)
            high(0, 1)
            tokens_high(0)
            high(0, 2)
            for c in range(KT):
                act.wait_ge(S("accb_done"), c + 1)
                cp(acc[:, c, :], banks[BIAS_BANKS[c % len(BIAS_BANKS)]][:, 0:NT]).then_inc(S("accb_ready"), 1)
            blocks(0, NPAIR)
            act.wait_ge(S("flag_ready"), 1)
            over_ = act.value_load(flagi[0:1, 0:1], min_val=0, max_val=1)
            with act.If(over_ > 0):
                blocks(NPAIR, NPAIR * NBLK)
            act.nop()
            norms(2, h, "yres_done")

        @block.vector
        def _(dve):
            v = nc.vector
            n = [0]

            def link(ins):
                n[0] += 1
                ins.then_inc(S("dve_chain"), 1)
                dve.wait_ge(S("dve_chain"), n[0])

            def signal(ins, name):
                ins.then_inc(S(name), 1)

            def wait_filled(stage, i):
                dve.wait_ge(S("unit_filled"), U(stage, i + 1))
                return bank(stage, i)

            def norm(k, src, dst, name):
                for tile_ in range(3):
                    r_, o_ = TN[tile_], st[0:TN[tile_], 3 * k + tile_:3 * k + tile_ + 1]
                    dve.wait_ge(S("rms"), 3 * k + tile_ + 1)
                    link(v.reciprocal(o_, o_))
                    last_ = v.scalar_tensor_tensor(out=dst[0:r_, tile_, :], in0=src[0:r_, tile_, :], scalar=o_, in1=gain[0:r_, :],
                                                   op0=ALU.mult, op1=ALU.mult)
                    signal(last_, name)
            b = wait_filled("params", 0)
            v.tensor_copy(par[:, :], b[:, 0:NPAR]).then_inc(S("params_ready"), 1)
            dve.wait_ge(S("params_ready"), 1)
            link(v.tensor_tensor(der[:, 0:4], par[:, 0:4], par[:, 4:8], ALU.subtract))
            v.tensor_scalar(der[:, 8:12], par[:, PR["ka"][0]:PR["ka"][0] + 4], -1.0, 1.0, ALU.mult, ALU.add)\
                .then_inc(S("par_ready"), 1)
            dve.wait_ge(S("gain_in"), 16)
            norm(0, h, h, "h_done")
            for c in range(KT):
                b = wait_filled("hT", c)
                signal(v.tensor_copy(hT[:, c, :], b[:, 0:NTP]), "hT_ready")
            dve.wait_ge(S("shift_out"), 16 * (NS + 1))
            dve.wait_ge(S("consts_ready"), 1)
            nraw, nmix = 0, 0

            def gate_tile(n_, j, buf):
                dve.wait_ge(S("proj_ready"), n_ + 1)
                v.scalar_tensor_tensor(out=hg[:, j - 12, :], in0=hg[:, j - 12, :], scalar=pcol("gnw"),
                                       in1=raw[:, buf, 0:NT], op0=ALU.mult, op1=ALU.mult).then_inc(S("raw_used"), 1)
            for n_, (j, _, _) in enumerate(PROJ[:len(PROJ) - LATE]):
                dve.wait_ge(S("proj_ready"), n_ + 1)
                if j < 4 or 12 <= j < 16:
                    if j < 4:
                        signal(v.tensor_tensor(hq[:, j, :], hq[:, j, :], raw[:, nraw % 2, 0:NT], ALU.mult), "raw_used")
                    else:
                        gate_tile(n_, j, nraw % 2)
                    nraw += 1
                elif j < 8:
                    dve.wait_ge(S("lb_ready"), 1)
                    if j == 4:
                        link(v.tensor_scalar(der[:, 4:8], der[:, 0:4], -1.0, 1.0, ALU.mult, ALU.add))
                    i = j - 4
                    link(v.tensor_scalar(hf[:, i, :], hf[:, i, :], der[:, 4 + i:5 + i], der[:, i:i + 1], ALU.mult, ALU.add))
                    signal(v.tensor_scalar(hk[:, i, :], hf[:, i, :], -1.0, 1.0, ALU.mult, ALU.add), "hk_ready")
                elif j >= 16:
                    r_ = raw[:, nraw % 2, :]
                    dve.wait_ge(S("dve_chain"), n[0])
                    v.tensor_tensor(dif[:, 1:NT], r_[:, 0:NT - 1], r_[:, 1:NT], ALU.subtract)
                    link(v.tensor_scalar(dif[:, 0:1], r_[:, 0:1], -1.0, None, ALU.mult))
                    link(v.tensor_tensor(dif[:, NP_:NT:TS], r_[:, NT:NTP], r_[:, NP_:NT:TS], ALU.subtract))
                    dst = {4: rr, 5: rk, 6: rv}[j // 4][:, j % 4, :] if j < 28 else lor[:, j - 28, :]
                    ins = v.scalar_tensor_tensor(out=dst, in0=dif[:, :], scalar=pcol("mu", j - 16), in1=r_[:, 0:NT],
                                                 op0=ALU.mult, op1=ALU.add)
                    ins.then_inc(S("raw_used"), 1)
                    nraw += 1
                    dve.wait_ge(S("raw_used"), nraw)
                    if j >= 28:
                        link(v.memset(st[0:1, 15:16], 0.0))
                        v.memset(st[0:1, 15:16], 0.0).then_inc(S("lor_ready"), 1)
                    nmix += 1
                    if nmix == 14:
                        v.memset(st[0:1, 14:15], 0.0).then_inc(S("mixed"), 14)
                if n_ == 13:
                    dve.wait_ge(S("wpre_ready"), 4)
                    dve.wait_ge(S("consts_ready"), 1)
                    for i in range(4):
                        ins = v.tensor_tensor_scan(tA[:, i, :], reset[:, :], rs[:, i, :], 0.0, ALU.mult, ALU.add)
                    link(ins)
                    link(v.tensor_tensor(rs[:, :, :], tA[:, :, :], rs[:, :, :], ALU.subtract))
                    for i in range(2):
                        ins = v.tensor_copy(cen[:, i, :], tA[:, :, P * i + 63])
                    link(ins)
                    for i in range(2):
                        w = slice(P * i, P * i + P)
                        v.tensor_tensor(tA[:, :, w], tA[:, :, w], bc(cen[:, i, :], P), ALU.subtract)
                        ins = v.tensor_tensor(rs[:, :, w], rs[:, :, w], bc(cen[:, i, :], P), ALU.subtract)
                    link(ins)
                    v.memset(st[0:1, 14:15], 0.0).then_inc(S("cen_ready"), 1)
                    v.memset(st[0:1, 13:14], 0.0).then_inc(S("gs_ready"), 1)
                if n_ == 21:
                    dve.wait_ge(S("kss_ready"), 1)
                    for r_, a_, z_ in ((P, 0, 16), (64, 16, 24)):
                        link(v.tensor_scalar(nrm[0:r_, 0, a_:z_], nrm[0:r_, 0, a_:z_], 1e-12, None, ALU.max))
                        ins = v.reciprocal(nrm[0:r_, 1, a_:z_], nrm[0:r_, 0, a_:z_])
                    signal(ins, "kinv_ready")
                if n_ == 25:
                    dve.wait_ge(S("apre_ready"), 4)
                    for i in range(4):
                        b = wait_filled("knb", i)
                        ins = v.scalar_tensor_tensor(out=rkk[:, i, :], in0=rk[:, i, :], scalar=pcol("kk", i), in1=b[:, 0:NT],
                                                     op0=ALU.mult, op1=ALU.mult)
                        signal(ins, "knb_ready")
                        link(v.tensor_scalar(rbon[:, i, :], ra[:, i, :], pcol("ka", i), der[:, 8 + i:9 + i], ALU.mult, ALU.add))
                        link(v.tensor_tensor(rk[:, i, :], rk[:, i, :], rbon[:, i, :], ALU.mult))
                        ins = v.scalar_tensor_tensor(out=rbon[:, i, :], in0=rr[:, i, :], scalar=pcol("rk", i), in1=rk[:, i, :],
                                                     op0=ALU.mult, op1=ALU.mult)
                        signal(ins, "rbon_in")
            dve.wait_ge(S("raw_used"), nraw)
            dve.wait_ge(S("hk_ready"), 4)
            link(v.memset(at_[:, :], 0.0))
            signal(v.memset(st[0:1, 14:15], 0.0), "at_zero")
            at, seen = 0, 0
            order = LEVELS + [0]
            for i, hh in enumerate(order):
                if i:
                    dve.wait_ge(S("unit_filled"), U("lvl", at))
                if hh:
                    if i:
                        dve.wait_ge(S("pre_ready"), i)
                    v.tensor_tensor(qp[:, :, :], hq[:, :, :], hf[:, :, :], ALU.mult).then_inc(S("qp_ready"), 1)
                    dve.wait_ge(S("suf_ready"), i + 1)
                    dve.wait_ge(S("qp_ready"), i + 1)
                    m = npair(hh)
                    for j in range(4):
                        fv = hf[:, j, 0:m].rearrange("p (b a c) -> p b a c", a=2, c=hh)
                        ins = v.tensor_tensor(fv[:, :, 1, :], fv[:, :, 1, :],
                                              fv[:, :, 0, hh - 1:hh].broadcast_to([P, m // (2 * hh), hh]), ALU.mult)
                    ins.then_inc(S("pre_ready"), 1)
                for tile in range(3 if hh <= 4 else 2):
                    tn = TN[tile]
                    b = wait_filled("lvl", at)
                    msk_ = mT[0:tn, i, 0:tn] if hh else ident[0:tn, 0:tn]
                    if i:
                        dve.wait_ge(S("lvl_ready"), seen)
                    o = at_[0:tn, 512 * tile:512 * tile + 4 * tn].rearrange("p (j t) -> p j t", t=tn)
                    signal(v.copy_predicated(o, rep(msk_.bitcast(I32), 4), b[0:tn, 0:4 * tn].rearrange("p (j t) -> p j t", t=tn)),
                           "lvl_ready")
                    at += 1
                seen = at
                if 1 <= i <= LATE:
                    n_ = len(PROJ) - LATE + i - 1
                    gate_tile(n_, PROJ[n_][0], nraw % 2)
                    nraw += 1
            dve.wait_ge(S("raw_used"), nraw)
            dve.wait_ge(S("lvl_ready"), at)
            dve.wait_ge(S("pre_ready"), 7)
            v.memset(st[0:1, 14:15], 0.0).then_inc(S("at_ready"), 1)
            v.tensor_tensor(qp[:, :, :], hq[:, :, :], hf[:, :, :], ALU.mult).then_inc(S("qp_ready"), 1)
            dve.wait_ge(S("knb_ready"), 4)
            link(v.tensor_tensor(ra[:, :, :], ra[:, :, :], rkk[:, :, :], ALU.mult))
            dve.wait_ge(S("e3_ready"), 1)
            v.tensor_tensor(ra[:, :, :], ra[:, :, :], tB[:, :, :], ALU.mult)
            v.tensor_tensor(rk[:, :, :], rk[:, :, :], tB[:, :, :], ALU.mult)
            v.scalar_tensor_tensor(out=rkk[:, :, :], in0=rkk[:, :, :], scalar=-1.0, in1=rs[:, :, :],
                                   op0=ALU.mult, op1=ALU.mult)
            dve.wait_ge(S("e1_ready"), 1)
            dve.wait_ge(S("rbon_in"), 4)
            v.tensor_tensor(rr[:, :, :], rr[:, :, :], tA[:, :, :], ALU.mult)
            for i in range(2):
                v.tensor_copy(pc[:, :, i], tA[:, :, P * i + P - 1])
            ins = v.tensor_copy(pc[:, :, 2:10], tA[:, :, NP_ + TS - 1:NT:TS])
            link(ins)
            v.tensor_tensor(ec[:, 4:8], pc[:, :, 0], ec[:, 0:4], ALU.mult).then_inc(S("rw_ready"), 1)
            b = wait_filled("hs2", 0)
            dve.wait_ge(S("unit_filled"), U("ho", 2))
            dve.wait_ge(S("hs1_ready"), 1)
            link(v.tensor_tensor(hs[:, :, :], hs[:, :, :], bc(hf[:, :, NP_ - 1], P), ALU.mult))
            signal(v.tensor_tensor(hs[:, :, :], hs[:, :, :], b[:, :].rearrange("p (h v) -> p h v", v=P), ALU.add), "hs2_ready")
            dve.wait_ge(S("unit_filled"), U("ho", 3))
            for j in range(HGH):
                for half in range(2):
                    o = hs0[:, 4 * half:4 * half + 4, j, :]
                    t0 = NP_ + TS * 4 * half + TS - 1
                    link(v.tensor_tensor(o, o, bc(hf[:, j, t0:t0 + 3 * TS + 1:TS], P), ALU.mult))
                    b = wait_filled("hsend", 2 * j + half)
                    signal(v.tensor_tensor(o, o, b[:, :].rearrange("p (b v) -> p b v", v=P), ALU.add), "hsend_ready")
            dve.wait_ge(S("hvar_ready"), 1)
            v.reciprocal(nrm[:, 2, 0:8], nrm[:, 2, 0:8])
            signal(v.reciprocal(nrm[0:64, 2, 8:12], nrm[0:64, 2, 8:12]), "oinv_ready")
            for j in range(4):
                b = wait_filled("hvarb", j)
                ins = v.tensor_tensor(hq[:, j, :], hq[:, j, :], b[:, 0:NT], ALU.mult)
                signal(ins, "hvarb_ready")
            dve.wait_ge(S("hvarb_ready"), 4)
            v.tensor_tensor(hq[:, :, :], hq[:, :, :], hg[:, :, :], ALU.mult).then_inc(S("mix_hg"), 1)
            for j in range(4):
                b = wait_filled("bonus", j)
                signal(v.tensor_tensor(rbon[:, j, :], rv[:, j, :], b[:, 0:NT], ALU.mult), "bonus_ready")
            dve.wait_ge(S("hgrn_out"), 32)
            dve.wait_ge(S("mix_hg"), 1)
            for stage, dst, m128, m64 in (("gN", mW_, mT[:, 0, :], mT[0:64, 0, 0:64]), ("gK", mK_, strict, strict8),
                                          ("gRb", mRb_, incl, incl8), ("gRk", mRk_, incl, incl8)):
                for x in range(6):
                    tile, p = x // 2, x % 2
                    tn = TN[tile]
                    b = wait_filled(stage, x)
                    m_ = rep((m64 if tile == 2 else m128)[0:tn, 0:tn], 4)
                    ins = v.tensor_tensor(dst(tile, p), b[0:tn, 0:4 * tn].rearrange("p (j t) -> p j t", t=tn), m_, ALU.mult)
                    if stage == "gN":
                        link(ins)
                        ins = v.tensor_tensor(dst(tile, p), dst(tile, p), rep(ident[0:tn, 0:tn], 4), ALU.add)
                    signal(ins, f"{stage}_ready")
            done = {"mZ": 0, "mW": 0, "mT": 0}
            for i, hh in enumerate(LEVELS):
                if hh == 1:
                    continue
                units = [(tile, p) for tile in range(3 if hh <= 4 else 2) for p in range(2)]
                for stage, dst in (("mZ", mZ_), ("mW", mW_), ("mT", mT_)):
                    if stage == "mT" and hh == 64:
                        continue
                    for tile, p in units:
                        tn = TN[tile]
                        b = wait_filled(stage, done[stage])
                        src = b[0:tn, 0:4 * tn].rearrange("p (j t) -> p j t", t=tn)
                        if stage == "mZ":
                            if done["mT"]:
                                dve.wait_ge(S("unit_filled"), U("mT", done["mT"]))
                            ins = v.tensor_tensor(dst(tile, p), src, rep(mT[0:tn, i, 0:tn], 4), ALU.mult)
                        else:
                            if stage == "mW":
                                dve.wait_ge(S("gN_ready"), 6)
                                if done["mW"]:
                                    dve.wait_ge(S("mW_ready"), done["mW"])
                            else:
                                dve.wait_ge(S("T1_ready"), 6)
                                if done["mT"]:
                                    dve.wait_ge(S("mT_ready"), done["mT"])
                            ins = v.tensor_tensor(dst(tile, p), dst(tile, p), src, ALU.add)
                        signal(ins, f"{stage}_ready")
                        done[stage] += 1
            for tile in range(2):
                for p in range(2):
                    rows = slice(64 * p, 64 * p + 64)
                    b = wait_filled("S", 2 * tile + p)
                    o = sp[rows, :].rearrange("p (j v) -> p j v", v=RN)
                    src = b[rows, 0:256].rearrange("p (j v) -> p j v", v=RN)
                    if tile == 0:
                        ins = v.tensor_tensor(o, src, bc(ec[rows, 4:8], RN), ALU.mult)
                    else:
                        dve.wait_ge(S("unit_filled"), U("Y", 4))
                        dve.wait_ge(S("S_ready"), 2)
                        link(v.tensor_tensor(o, o, src, ALU.add))
                        ins = v.tensor_tensor(o, o, bc(pc[rows, :, 1], RN), ALU.mult)
                    signal(ins, "S_ready")
            dve.wait_ge(S("U_ready"), 6)
            for x in range(RWH):
                if x >= 2:
                    dve.wait_ge(*half_done(x - 2))
                v.tensor_tensor(um[0:64, x % 2], rep(uu[0:64, 2, RN * x:RN * x + RN], NS), bc(seqm[:, :], RN), ALU.mult)\
                    .then_inc(S("um_ready"), 1)
            dve.wait_ge(S("unit_filled"), U("Y", 6))
            dve.wait_ge(S("s0t_ready"), 4)
            for j in range(4):
                b = wait_filled("send", j)
                for q in range(4):
                    o = s0t[:, q, j]
                    ins = v.tensor_tensor(o, o, b[:, P * q:P * q + P].rearrange("p (c v) -> p c v", v=RN), ALU.add)
                link(ins)
                for q in range(4):
                    o = s0t[:, q, j]
                    ins = v.tensor_tensor(o, o, bc(pc[:, j, 2 + 2 * q:4 + 2 * q], RN), ALU.mult)
                signal(ins, "send_ready")
            dve.wait_ge(S("Y_ready"), 6)
            for j in range(4):
                b = wait_filled("mean", j)
                ins = v.tensor_tensor(yy[:, j, :], yy[:, j, :], b[:, 0:NT], ALU.subtract)
                signal(ins, "mean_ready")
            dve.wait_ge(S("mean_ready"), 4)
            v.memset(st[0:1, 14:15], 0.0).then_inc(S("yc_ready"), 4)
            dve.wait_ge(S("var_ready"), 1)
            v.reciprocal(nrm[:, 3, 0:16], nrm[:, 2, 0:16])
            signal(v.reciprocal(nrm[0:64, 3, 16:24], nrm[0:64, 2, 16:24]), "yinv_ready")
            dve.wait_ge(S("bonus_ready"), 4)
            dve.wait_ge(S("gpre_ready"), 4)
            for j in range(4):
                b = wait_filled("varb", j)
                ins = v.tensor_tensor(yy[:, j, :], yy[:, j, :], b[:, 0:NT], ALU.mult)
                signal(ins, "varb_ready")
                dve.wait_ge(S("varb_ready"), j + 1)
                link(v.tensor_scalar(yy[:, j, :], yy[:, j, :], pcol("lnw", j), pcol("lnb", j), ALU.mult, ALU.add))
            link(v.tensor_tensor(yy[:, :, :], yy[:, :, :], rbon[:, :, :], ALU.add))
            v.tensor_tensor(yy[:, :, :], yy[:, :, :], rg[:, :, :], ALU.mult).then_inc(S("mixer_done"), 1)
            dve.wait_ge(S("xres_in"), 48)
            for x in range(6):
                tn, tile, half = TN[x // 2], x // 2, x % 2
                b = wait_filled("xo", x)
                o = h[0:tn, tile, 512 * half:512 * half + 512]
                signal(v.tensor_tensor(o, o, b[0:tn, :], ALU.add), "xo_ready")
            dve.wait_ge(S("xo_ready"), 6)
            dve.wait_ge(S("gain2_in"), 16)
            norm(1, h, h2, "h2_done")
            v.tensor_tensor(twin[:, :], ident[:, 0:CAP], ident[:, CAP:P], ALU.add).then_inc(S("twin_ready"), 1)
            for c in range(KT):
                b = wait_filled("h2T", c)
                signal(v.tensor_copy(hT[:, c, 0:NT], b[:, 0:NT]), "h2T_ready")
            b = wait_filled("logit", 0)
            dve.wait_ge(S("router_in"), 32)
            for tile in range(3):
                tn = TN[tile]
                ins = v.tensor_tensor(lgt[0:tn, tile, :], b[0:tn, NE * tile:NE * tile + NE], brow[0:tn, :], ALU.add)
            signal(ins, "logit_ready")
            dve.wait_ge(S("logit_ready"), 1)
            for tile in range(3):
                tn = TN[tile]
                link(v.max(top[0:tn, tile, :], lgt[0:tn, tile, :]))
                link(v.max_index(topi[0:tn, tile, :], top[0:tn, tile, :], lgt[0:tn, tile, :]))
                v.tensor_copy(topf[0:tn, tile, :], topi[0:tn, tile, :])
                ins = v.tensor_scalar(gat[0:tn, tile, 0:4], top[0:tn, tile, 0:4], top[0:tn, tile, 0:1], None, ALU.subtract)
                signal(ins, "top_ready")
            dve.wait_ge(S("top_exp"), 3)
            for tile in range(3):
                tn = TN[tile]
                link(v.tensor_reduce(gat[0:tn, tile, 4:5], gat[0:tn, tile, 0:4], AX.X, ALU.add))
                link(v.reciprocal(gat[0:tn, tile, 5:6], gat[0:tn, tile, 4:5]))
                link(v.tensor_scalar(gat[0:tn, tile, 0:4], gat[0:tn, tile, 0:4], gat[0:tn, tile, 5:6], None, ALU.mult))
                for q in range(TOPK):
                    ids, gcol = topf[0:tn, tile, q:q + 1], gat[0:tn, tile, q:q + 1]
                    if q == 0:
                        v.tensor_scalar(msk[0:tn, tile, :], iota[0:tn, 0:NE], ids, None, ALU.is_equal)
                        link(v.tensor_scalar(gate[0:tn, tile, 0:NE], iota[0:tn, 0:NE], ids, gcol, ALU.is_equal, ALU.mult))
                    else:
                        link(v.tensor_scalar(hot[0:tn, :], iota[0:tn, 0:NE], ids, None, ALU.is_equal))
                        v.tensor_tensor(msk[0:tn, tile, :], msk[0:tn, tile, :], hot[0:tn, :], ALU.add)
                        link(v.scalar_tensor_tensor(out=gate[0:tn, tile, 0:NE], in0=hot[0:tn, :], scalar=gcol,
                                                    in1=gate[0:tn, tile, 0:NE], op0=ALU.mult, op1=ALU.add))
                v.memset(st[0:1, 14:15], 0.0).then_inc(S("msk_ready"), 1)
            b = wait_filled("rank", 0)
            for tile in range(3):
                tn = TN[tile]
                link(v.scalar_tensor_tensor(out=rnk[0:tn, tile, 0:NE], in0=msk[0:tn, tile, :], scalar=-FAR,
                                            in1=b[0:tn, NE * tile:NE * tile + NE], op0=ALU.mult, op1=ALU.add))
                link(v.tensor_scalar(rnk[0:tn, tile, 0:NE], rnk[0:tn, tile, 0:NE], FAR, None, ALU.add))
            v.tensor_reduce(flag[0:1, 0:1], b[0:1, 96:96 + NE], AX.X, ALU.max).then_inc(S("rank_ready"), 1)
            dve.wait_ge(S("rank_ready"), 1)
            link(v.tensor_scalar(flag[0:1, 1:2], flag[0:1, 0:1], CAP + 0.5, None, ALU.is_gt))
            v.tensor_copy(flagi[0:1, 0:1], flag[0:1, 1:2]).then_inc(S("flag_ready"), 1)

            def select(k):
                for tile_ in range(3):
                    tn_ = TN[tile_]
                    for s in range(2):
                        last_ = v.tensor_scalar(sel[0:tn_, tile_, CAP * s:CAP * s + CAP],
                                                iota[0:tn_, bass.ds((k >> 4) * CAP, CAP)],
                                                rnk[0:tn_, tile_, bass.ds((k & (NPAIR - 1)) * 2 + s, 1)], None, ALU.is_equal)
                signal(last_, "sel_ready")

            def select_gates(e):
                dve.wait_ge(S("selg_turned"), e)
                x = e & (NE - 1)
                for tile_ in range(3):
                    tn_ = TN[tile_]
                    last_ = v.tensor_scalar(selg[0:tn_, tile_, :, :], rep(iota[0:tn_, bass.ds((e >> 5) * CAP, CAP)], 2),
                                            rnk[0:tn_, tile_, bass.ds(x, 1)], gate[0:tn_, tile_, bass.ds(x, 1)],
                                            ALU.is_equal, ALU.mult)
                signal(last_, "selg_ready")

            def low(k, i):
                dve.wait_ge(S("hi_ready"), 2 * NPC * k + i + 1)
                if not (isinstance(k, int) and k == 0 and i < NLO):
                    dve.wait_ge(S("w_used"), 2 * NPC * k + i - NLO + 1)
                v.tensor_tensor(wlo[i % NLO][:, 0:3, :], w32[i % NW][:, 0:3, :], whi[i % NHI][:, 0:3, :].bitcast(F32),
                                ALU.subtract).then_inc(S("lo_ready"), 1)

            def tokens_low(k):
                dve.wait_ge(S("xg_high"), k + 1)
                for i in range(2):
                    for ab in range(2):
                        b_ = banks[4 + i][:, :].rearrange("p (c b s) -> p c b s", b=2, s=CAP)[:, :, ab, :]
                        last_ = v.tensor_tensor(xg[:, 4 * i:4 * i + 4, ab, 1, :], b_,
                                                xg[:, 4 * i:4 * i + 4, ab, 0, :].bitcast(F32), ALU.subtract)
                last_.then_inc(S("xg_ready"), 1)

            def swiglu(e, i):
                ex = e & (NE - 1)
                cs, n = slice(4 * i, 4 * i + 4), 2 * e + i
                bs = slice(4 * i * CAP, 4 * (i + 1) * CAP)
                dve.wait_ge(S("combined"), 4 * e + 2 * (i + 1))
                dve.wait_ge(S("h1_ready"), n)
                v.tensor_tensor(gg[:, cs, :], banks[2][:, bs].rearrange("p (c s) -> p c s", s=CAP),
                                bc(bgu[:, bass.ds(ex * 16 + 4 * i, 4)], CAP), ALU.add).then_inc(S("g1"), 1)
                v.tensor_tensor(upv[:, cs, :], banks[3][:, bs].rearrange("p (c s) -> p c s", s=CAP),
                                bc(bgu[:, bass.ds(ex * 16 + 8 + 4 * i, 4)], CAP), ALU.add).then_inc(S("gu_read"), 1)
                dve.wait_ge(S("g1"), n + 1)
                v.tensor_scalar(gg[:, cs, :], gg[:, cs, :], LIMIT, None, ALU.min).then_inc(S("gate_ready"), 1)
                dve.wait_ge(S("gu_read"), n + 1)
                v.tensor_scalar(upv[:, cs, :], upv[:, cs, :], LIMIT, -LIMIT, ALU.min, ALU.max).then_inc(S("up_clip"), 1)
                dve.wait_ge(S("sig_ready"), n + 1)
                dve.wait_ge(S("gate_ready"), n + 1)
                v.tensor_tensor(gg[:, cs, :], gg[:, cs, :], sg[:, cs, :], ALU.mult).then_inc(S("glu_done"), 1)
                dve.wait_ge(S("glu_done"), n + 1)
                dve.wait_ge(S("up_clip"), n + 1)
                v.scalar_tensor_tensor(out=gg[:, cs, :], in0=upv[:, cs, :], scalar=1.0, in1=gg[:, cs, :],
                                       op0=ALU.add, op1=ALU.mult).then_inc(S("hidden"), 1)
                dve.wait_ge(S("hidden"), n + 1)
                if not (isinstance(e, int) and e == 0):
                    dve.wait_ge(S("w_used"), e * NPC)
                v.tensor_copy(h1[:, cs, 0, :], gg[:, cs, :]).then_inc(S("h1_high"), 1)
                dve.wait_ge(S("h1_high"), n + 1)
                v.tensor_tensor(h1[:, cs, 1, :], gg[:, cs, :], h1[:, cs, 0, :].bitcast(F32), ALU.subtract)\
                    .then_inc(S("h1_ready"), 1)

            def add_up(e, c0):
                for c in (c0, c0 + 1):
                    dve.wait_ge(S("scattered"), 8 * e + c + 1)
                    v.tensor_tensor(acc[:, c, :], acc[:, c, :], banks[6 + c % 2][:, 0:NT], ALU.add).then_inc(S("acc_added"), 1)

            def pair(k, before, last):
                for ab in range(2):
                    e = k * 2 + ab
                    for i in range(NPC):
                        ahead = NPC * ab + i + NHI - 2
                        if not last or ahead < 2 * NPC:
                            low(k, ahead)
                        if i == 5:
                            swiglu(e, 0)
                        if (before or ab) and 6 <= i <= 8:
                            add_up(e - 1, 2 * (i - 6))
                        if i == 8:
                            swiglu(e, 1)
                            if before or ab:
                                add_up(e - 1, 6)
                        if i == 9 and ab:
                            tokens_low(k + 1)
                        if i == 10:
                            select_gates(e)
                        if i == 10 and ab:
                            dve.wait_ge(S("gathered"), 2 * k + 4)
                            select(k + 2)

            def blocks(k0, k1):
                if k0:
                    for i in range(NHI - 2):
                        low(k0, i)
                pair(k0, False, False)
                with dve.Fori(k0 + 1, k1 - 1) as k:
                    pair(k, True, False)
                pair(k1 - 1, True, True)
                for c0 in range(0, KT, 2):
                    add_up(2 * k1 - 1, c0)
            select(0)
            low(0, 0)
            low(0, 1)
            tokens_low(0)
            select(1)
            dve.wait_ge(S("accb_ready"), KT)
            blocks(0, NPAIR)
            over_ = dve.value_load(flagi[0:1, 0:1], min_val=0, max_val=1)
            with dve.If(over_ > 0):
                blocks(NPAIR, NPAIR * NBLK)
            dve.nop()
            v.memset(st[0:1, 14:15], 0.0).then_inc(S("acc_done"), 1)
            for tile in range(3):
                tn = TN[tile]
                dve.wait_ge(S("acc_turned"), tile + 1)
                for i in range(2):
                    o = h[0:tn, tile, 512 * i:512 * i + 512]
                    v.tensor_tensor(o, o, banks[2 * tile + i][0:tn, :], ALU.add).then_inc(S("yres_done"), 1)
            dve.wait_ge(S("gain3_in"), 16)
            norm(2, h, yrow, "y_done")


_INS = ["x_prompt", "x_sample", "state_hgrn", "state_rwkv", "state_shift", "norm_mix", "w_in", "lb_logits", "hg_norm_w",
        "rw_mu", "rw_w0", "rw_w2", "rw_a0", "rw_a2", "rw_g2", "rw_k_k", "rw_k_a", "rw_r_k", "rw_lnx_w", "rw_lnx_b",
        "w_out", "norm_ffn", "w_router", "b_router", "w_gate_up", "b_gate_up", "w_down", "b_down", "norm_final"]
_OUTS = [(1, NP_, DM), (NS, TS, DM), (1, 1, HGH, P, P), (1, 1, RWH, RN, RN), (1, 1, DM),
         (1, NS, HGH, P, P), (1, NS, RWH, RN, RN), (1, NS, DM)]


def kernel(**inputs):
    import numpy as _np
    import concourse.bacc as _bacc
    from concourse import mybir as _mybir
    from concourse.bass_utils import run_bass_kernel_spmd as _run

    nc = _bacc.Bacc("TRN2", target_bir_lowering=False, num_devices=1)
    arrays, ins = {}, {}
    for name in _INS:
        a = _np.ascontiguousarray(inputs[name])
        arrays[f"in_{name}"] = a
        ins[name] = nc.dram_tensor(f"in_{name}", a.shape, _mybir.dt.from_np(a.dtype), kind="ExternalInput").ap()
    outs = [nc.dram_tensor(f"out_{i}", s, _mybir.dt.float32, kind="ExternalOutput").ap() for i, s in enumerate(_OUTS)]
    build(nc, ins, outs)
    r = _run(nc, [arrays], core_ids=[0])
    return tuple(r.results[0][f"out_{i}"] for i in range(len(_OUTS)))
```
